# Optimizing a Trainium2 kernel written in Bass

```python
import math
import jax, jax.numpy as jnp
from jax import lax
import numpy as np

'''Bidirectional hybrid encoder trunk: interleaved differential-attention / short-gated-conv layers, each followed by a gated ConvFFN.
Inputs: x (BATCH, SEQ, D_MODEL) float32, positions (BATCH, SEQ) int32, stacked per-layer parameters.
Output: (BATCH, SEQ, D_MODEL) after a final RMSNorm.'''

D_MODEL = 1024
BATCH = 1
SEQ = 1024
DEPTH = 2

N_MIXERS = 2
N_HEADS = 8
HEAD_DIM = 64
V_DIM = 2 * HEAD_DIM
Q_BLOCK = 128
ROPE_THETA = 10000.0
CONV_WIDTH = 3
D_FF = 2816
RMS_EPS = 1e-5
N_ATTN_LAYERS = (DEPTH + N_MIXERS - 1) // N_MIXERS
N_CONV_LAYERS = (DEPTH + N_MIXERS - 2) // N_MIXERS

kernel_name = 'hybrid_diffattn_shortconv_encoder'

def rms_norm(x, g):
    xf = x.astype(jnp.float32)
    y = xf * lax.rsqrt(jnp.mean(xf * xf, axis=-1, keepdims=True) + RMS_EPS)
    return (y * g.astype(jnp.float32)).astype(x.dtype)

def dwconv3(x, w):
    xp = jnp.pad(x, ((0, 0), (1, 1), (0, 0)))
    return xp[:, :-2] * w[0] + xp[:, 1:-1] * w[1] + xp[:, 2:] * w[2]

def rotary_cos_sin(positions, dim):
    inv_freq = ROPE_THETA ** (-jnp.arange(0, dim, 2, dtype=jnp.float32) / dim)
    ang = positions.astype(jnp.float32)[..., None] * inv_freq
    return jnp.cos(ang), jnp.sin(ang)

def apply_rotary(x, cos, sin):
    x1, x2 = jnp.split(x.astype(jnp.float32), 2, axis=-1)
    c = cos[:, :, None, :]
    s = sin[:, :, None, :]
    return jnp.concatenate([x1 * c - x2 * s, x2 * c + x1 * s], axis=-1).astype(x.dtype)

def diff_attention(h, positions, w_qkv, lq1, lk1, lq2, lk2, subln_g, w_o, lambda_init):
    B, S, _ = h.shape
    q, k, v = jnp.split(h @ w_qkv, 3, axis=-1)
    q = q.reshape(B, S, 2 * N_HEADS, HEAD_DIM)
    k = k.reshape(B, S, 2 * N_HEADS, HEAD_DIM)
    v = v.reshape(B, S, N_HEADS, V_DIM)
    cos, sin = rotary_cos_sin(positions, HEAD_DIM)
    q = apply_rotary(q, cos, sin) * (HEAD_DIM ** -0.5)
    k = apply_rotary(k, cos, sin)
    q = q.reshape(B, S, N_HEADS, 2, HEAD_DIM)
    k = k.reshape(B, S, N_HEADS, 2, HEAD_DIM)
    lq1f, lk1f = lq1.astype(jnp.float32), lk1.astype(jnp.float32)
    lq2f, lk2f = lq2.astype(jnp.float32), lk2.astype(jnp.float32)
    lam = jnp.exp(jnp.sum(lq1f * lk1f)) - jnp.exp(jnp.sum(lq2f * lk2f)) + lambda_init
    nb = S // Q_BLOCK
    qb = q.reshape(B, nb, Q_BLOCK, N_HEADS, 2, HEAD_DIM).transpose(1, 0, 2, 3, 4, 5)

    def attend(q_blk):
        s = jnp.einsum('bqhcd,bkhcd->bhcqk', q_blk, k, preferred_element_type=jnp.float32)
        p = jax.nn.softmax(s, axis=-1)
        a = p[:, :, 0] - lam * p[:, :, 1]
        return jnp.einsum('bhqk,bkhe->bqhe', a.astype(v.dtype), v)

    o = lax.map(attend, qb)
    o = o.transpose(1, 0, 2, 3, 4).reshape(B, S, N_HEADS, V_DIM)
    o = rms_norm(o, subln_g) * (1.0 - lambda_init)
    return o.reshape(B, S, N_HEADS * V_DIM) @ w_o

def short_conv_mixer(h, w_in, conv_w, w_out):
    b, c, u = jnp.split(h @ w_in, 3, axis=-1)
    return (b * dwconv3(c * u, conv_w)) @ w_out

def conv_ffn(h, w_up, conv_w, conv_b, w_down):
    u = dwconv3(h @ w_up, conv_w) + conv_b
    gate, val = jnp.split(u, 2, axis=-1)
    return (jax.nn.silu(gate) * val) @ w_down

def setup_inputs(seed: int = 0) -> dict:
    key = jax.random.key(seed)
    ks = jax.random.split(key, 24)

    def nrm(k, shape, scale):
        return jax.random.normal(k, shape, dtype=jnp.float32) * scale

    NA, NC, L = N_ATTN_LAYERS, N_CONV_LAYERS, DEPTH
    x = nrm(ks[0], (BATCH, SEQ, D_MODEL), 1.0)
    positions = jnp.broadcast_to(jnp.arange(SEQ, dtype=jnp.int32), (BATCH, SEQ))
    return {
        'x': x,
        'positions': positions,
        'attn_norm_g': 1.0 + nrm(ks[1], (NA, D_MODEL), 0.02),
        'attn_w_qkv': nrm(ks[2], (NA, D_MODEL, 3 * D_MODEL), D_MODEL ** -0.5),
        'attn_lambda_q1': nrm(ks[3], (NA, HEAD_DIM), 0.1),
        'attn_lambda_k1': nrm(ks[4], (NA, HEAD_DIM), 0.1),
        'attn_lambda_q2': nrm(ks[5], (NA, HEAD_DIM), 0.1),
        'attn_lambda_k2': nrm(ks[6], (NA, HEAD_DIM), 0.1),
        'attn_subln_g': 1.0 + nrm(ks[7], (NA, V_DIM), 0.02),
        'attn_w_o': nrm(ks[8], (NA, D_MODEL, D_MODEL), D_MODEL ** -0.5),
        'conv_norm_g': 1.0 + nrm(ks[9], (NC, D_MODEL), 0.02),
        'conv_w_in': nrm(ks[10], (NC, D_MODEL, 3 * D_MODEL), D_MODEL ** -0.5),
        'conv_w': nrm(ks[11], (NC, CONV_WIDTH, D_MODEL), CONV_WIDTH ** -0.5),
        'conv_w_out': nrm(ks[12], (NC, D_MODEL, D_MODEL), D_MODEL ** -0.5),
        'ffn_norm_g': 1.0 + nrm(ks[13], (L, D_MODEL), 0.02),
        'ffn_w_up': nrm(ks[14], (L, D_MODEL, 2 * D_FF), D_MODEL ** -0.5),
        'ffn_conv_w': nrm(ks[15], (L, CONV_WIDTH, 2 * D_FF), CONV_WIDTH ** -0.5),
        'ffn_conv_b': nrm(ks[16], (L, 2 * D_FF), 0.02),
        'ffn_w_down': nrm(ks[17], (L, D_FF, D_MODEL), D_FF ** -0.5),
        'final_norm_g': 1.0 + nrm(ks[18], (D_MODEL,), 0.02),
    }

def reference(x, positions, attn_norm_g, attn_w_qkv, attn_lambda_q1, attn_lambda_k1, attn_lambda_q2, attn_lambda_k2, attn_subln_g, attn_w_o, conv_norm_g, conv_w_in, conv_w, conv_w_out, ffn_norm_g, ffn_w_up, ffn_conv_w, ffn_conv_b, ffn_w_down, final_norm_g):
    for i in range(DEPTH):
        if i % N_MIXERS == 0:
            a = i // N_MIXERS
            lambda_init = 0.8 - 0.6 * math.exp(-0.3 * i)
            h = rms_norm(x, attn_norm_g[a])
            x = x + diff_attention(h, positions, attn_w_qkv[a], attn_lambda_q1[a], attn_lambda_k1[a],
                                   attn_lambda_q2[a], attn_lambda_k2[a], attn_subln_g[a], attn_w_o[a],
                                   lambda_init)
        else:
            c = i // N_MIXERS
            h = rms_norm(x, conv_norm_g[c])
            x = x + short_conv_mixer(h, conv_w_in[c], conv_w[c], conv_w_out[c])
        h = rms_norm(x, ffn_norm_g[i])
        x = x + conv_ffn(h, ffn_w_up[i], ffn_conv_w[i], ffn_conv_b[i], ffn_w_down[i])
    return rms_norm(x, final_norm_g)


_drawn_inputs = setup_inputs


def setup_inputs(seed=0):
    import zlib

    import numpy as np

    out = dict(_drawn_inputs(seed))
    spreads = {}
    factors = {'attn_lambda_q2': 35.789,
     'attn_subln_g': 2.86,
     'conv_norm_g': 2.721,
     'ffn_norm_g': 2.842,
     'ffn_conv_b': 2.929,
     'final_norm_g': 8.422}
    for name, (base, spread) in spreads.items():
        noise = np.random.default_rng([zlib.crc32(name.encode()), seed]).standard_normal(out[name].shape)
        drawn = base * np.exp(spread * noise) if base else spread * noise
        out[name] = __import__('jax').numpy.asarray(drawn.astype(out[name].dtype))
    for name, factor in factors.items():
        out[name] = (out[name] * factor).astype(out[name].dtype)
    return out
```

```python
from contextlib import ExitStack

import numpy as np

import concourse.bass as bass
from concourse import mybir

F32 = mybir.dt.float32
F32R = mybir.dt.float32r
I32 = mybir.dt.int32
ALU = mybir.AluOpType
ACT = mybir.ActivationFunctionType
AX_X = mybir.AxisListType.X

P = 128
D = 1024
S = 1024
KT = D // P
HALF = 512
DFF = 2816
FT = DFF // P
GROUPS = FT // 2
HEADS = 8
HD = 64
VD = 2 * HD
QT = S // P
EPS = 1e-5
THETA = 10000.0
LAMBDA_INIT = 0.2
SCALE = HD ** -0.5
MAGIC = 1.5 * 2.0 ** 23
TWO_PI = (6.28125, 0.0019350051879882812, 3.01991598196e-07)
PI_IN = 3.1415925

C_NORM = 0
C_FFN = C_NORM + 5 * KT
C_CONV = C_FFN + 2 * FT * 2 * 4
C_SUBG = C_CONV + KT * 3
N_PARAM = C_SUBG + 1

C_FREQ, C_SIGN, C_IDENT, C_EPSI = 0, 1, 2, 2 + P
N_CONST = 2 + 2 * P

T_QKV = 0
T_WO = T_QKV + 3 * HEADS
T_FFN0 = T_WO + KT
T_CIN = T_FFN0 + 2 * FT + 2 * GROUPS
T_COUT = T_CIN + 3 * KT
T_FFN1 = T_COUT + KT
T_END = T_FFN1 + 2 * FT + 2 * GROUPS


def wait(eng, sem, value):
    if isinstance(value, int) and value <= 0:
        return
    eng.wait_ge(sem, value)


def build(nc, x_in, positions, weights, params_in, consts_in, lams_in, out):
    ctx = ExitStack()
    with ctx:
        def sb(name, shape, dt=F32, stack=ctx):
            return stack.enter_context(nc.sbuf_tensor(name, shape, dt))

        def sem(name):
            return ctx.enter_context(nc.semaphore(name))

        q_dram = nc.dram_tensor("q_scratch", (HEADS, P, S), F32, kind="Internal").ap()
        k_dram = nc.dram_tensor("k_scratch", (HEADS, P, S), F32, kind="Internal").ap()
        v_dram = nc.dram_tensor("v_scratch", (HEADS, P, S), F32, kind="Internal").ap()

        X = sb("X", [P, KT, S])
        XGh = sb("XGh", [P, KT, S], F32R)
        XGl = sb("XGl", [P, KT, S], F32R)
        Wraw = sb("Wraw", [P, 2, 1024])
        Wh = sb("Wh", [P, 2, 1024], F32R)
        Wl = sb("Wl", [P, 2, 1024], F32R)
        R = sb("R", [P, S])
        acc = sb("acc", [P, S])
        sq = sb("sq", [P, 2, S])
        cu = sb("cu", [P, S + 2])
        par = sb("par", [P, N_PARAM])
        con = sb("con", [P, N_CONST])
        ones = sb("ones", [P, P])
        lam = sb("lam", [P, 8])
        mx = sb("mx", [P, 4])
        nb = sb("nb", [P, 4])
        rsum = sb("rsum", [P, 2, QT])
        coef = sb("coef", [P, 4])
        epsb = sb("epsb", [P, 1])
        with ExitStack() as one:
            Yh = sb("Yh", [P, KT, S], F32R, one)
            Yl = sb("Yl", [P, KT, S], F32R, one)
        with ExitStack() as two:
            Hh = sb("Hh", [P, 2, S], F32R, two)
            Hl = sb("Hl", [P, 2, S], F32R, two)
            rawg = sb("rawg", [P, S + 2], F32, two)
            rawv = sb("rawv", [P, S + 2], F32, two)
            Tg = sb("Tg", [P, S], F32, two)
            Tv = sb("Tv", [P, 2, S], F32, two)
        PS = ctx.enter_context(nc.psum_tensor("PS", [P, 4096], F32))
        ident = con[:, C_IDENT:C_IDENT + P]
        raws = (rawg, rawv)
        cos_r, sin_r, rot_a, rot_b, q_res, k_res, v_res, vt_res = (X[:, t, :] for t in range(KT))
        Pb = [[X[:, 2 * b + c, :] for c in range(2)] for b in range(2)]
        land = [X[:, 4 + r, :] for r in range(4)] + [acc[:, :]]
        Kh, Kl, Qs = ([XGh[:, 2 * t + c, :] for c in range(2)] for t in range(3))
        Vh, Vl = XGh[:, 6, :], XGh[:, 7, :]
        Ah = [XGl[:, 2 * b:2 * b + 2, :].rearrange("p a (t n) -> p (a t) n", n=2 * P) for b in range(2)]
        Al = [XGl[:, 4 + 2 * b:6 + 2 * b, :].rearrange("p a (t n) -> p (a t) n", n=2 * P) for b in range(2)]
        osq, osb, z, ot = (sq[:, 0, t * 2 * P:(t + 1) * 2 * P] for t in range(4))
        ot3 = sq[:, 0:1, 6 * P:8 * P]
        dg = cu[:, 0:4 * P]
        lams = cu[:, 0:4 * HD]

        def slot(s):
            return PS[:, s * 1024:(s + 1) * 1024]

        def gcol(norm, kt):
            return par[:, C_NORM + norm * KT + kt:C_NORM + norm * KT + kt + 1]

        w_in = [sem("w_in0"), sem("w_in1")]
        w_hi, w_lo = sem("w_hi"), sem("w_lo")
        x_in_sem = [sem(f"x_in{k}") for k in range(KT)]
        x_again = [sem(f"x_again{k}") for k in range(2)]
        small_in, ones_set, pos_in = sem("small_in"), sem("ones_set"), sem("pos_in")
        lam_ch = sem("lam_ch")
        stored = sem("stored")
        N = [dict(x=sem(f"n{n}_x_final"), hi=sem(f"n{n}_hi"), lo=sem(f"n{n}_lo"), sq=sem(f"n{n}_sq"),
                  used=sem(f"n{n}_sq_used"), sum=sem(f"n{n}_sum"), root=sem(f"n{n}_root"), r=sem(f"n{n}_r"))
             for n in range(5)]
        final_out = sem("final_out")
        qkv_done, v_out, rot_read, rot_sum = sem("qkv_done"), sem("v_out"), sem("rot_read"), sem("rot_sum")
        vt_done, vt_out, q_out, k_out = sem("vt_done"), sem("vt_out"), sem("q_out"), sem("k_out")
        q_st, k_st, v_st = sem("q_stored"), sem("k_stored"), sem("v_stored")
        tab, sin_done = sem("rotary_tables"), sem("sin_done")
        lam_sum, lam_exp, lam_done = sem("lam_sum"), sem("lam_exp"), sem("lam_done")
        land_in = [sem(f"landed{r}") for r in range(5)]
        kh_made, kl_made, qh_made, ql_made = sem("kh_made"), sem("kl_made"), sem("qh_made"), sem("ql_made")
        vh_made, vl_made = sem("vh_made"), sem("vl_made")
        s_done, mx_done, nb_done, e_done = sem("s_done"), sem("mx_done"), sem("nb_done"), sem("e_done")
        co_done, a_done, t_done = sem("coef_done"), sem("a_done"), sem("t_done")
        ah_made, al_made = sem("ah_made"), sem("al_made")
        s0sq_done, dg_done = sem("s0sq_done"), sem("dg_done")
        pv_done, o_copied, o_sq, ss_done = sem("pv_done"), sem("o_copied"), sem("o_squared"), sem("ss_done")
        ln_done, z_done, o_scaled = sem("ln_done"), sem("z_done"), sem("o_scaled")
        yh_made, yl_made = sem("yh_made"), sem("yl_made")
        dense_done = [sem("dense0_done"), sem("dense1_done")]
        c_done, c_free, cu_made, ct_mid, ct_made = (sem("conv_mm_done"), sem("conv_mm_free"), sem("cu_made"),
                                                    sem("ct_mid"), sem("ct_made"))
        cy_made, cyh, cyl, c_pad = sem("cy_made"), sem("cyh_made"), sem("cyl_made"), sem("conv_pad")
        F = [{k: sem(f"f{l}_{k}") for k in ("done", "free", "mid", "tap", "conv", "silu", "h", "hh", "hl", "pad")}
             for l in range(2)]

        block = ctx.enter_context(nc.Block())


        def load_tile(eng, n, s):
            wait(eng, w_lo, n - 1)
            eng.dma_start(Wraw[:, s, :], weights[bass.ds(n, 1)].rearrange("a p n -> p (a n)")).then_inc(w_in[s], 16)

        def split_hi(act, n_half, s, done, jobs):
            wait(act, done, jobs)
            act.wait_ge(w_in[s], 16 * (n_half + 1))
            act.activation(Wh[:, s, :], Wraw[:, s, :], ACT.Copy).then_inc(w_hi, 1)

        def split_lo(pool, n, s):
            pool.wait_ge(w_hi, n + 1)
            pool.tensor_tensor(Wl[:, s, :], Wraw[:, s, :], Wh[:, s, :].bitcast(F32), ALU.subtract).then_inc(w_lo, 1)

        def products(pe, ps, wh, wl, mh, ml, first, last):
            for w, m, begin in ((wh, mh, first), (wh, ml, False), (wl, mh, False)):
                for h in range(2):
                    ins = pe.matmul(ps[:, h * HALF:(h + 1) * HALF], w, m[:, h * HALF:(h + 1) * HALF],
                                    start=begin, stop=last and w is wl)
            return ins

        def full_job(pe, n, s, ps_slot, mh, ml, done, ready=None):
            pe.wait_ge(w_lo, n + 1)
            for kt in range(KT):
                if ready is not None:
                    pe.wait_ge(ready[0], kt + 1)
                    pe.wait_ge(ready[1], kt + 1)
                c = slice(kt * P, (kt + 1) * P)
                ins = products(pe, slot(ps_slot), Wh[:, s, c], Wl[:, s, c], mh[:, kt, :], ml[:, kt, :],
                               kt == 0, kt == KT - 1)
            ins.then_inc(done, 1)

        def square_sum(pe, n):
            pe.wait_ge(N[n]["used"], KT)
            for h in range(2):
                ins = pe.matmul(slot(3)[:, h * HALF:(h + 1) * HALF], ones[:, :], acc[:, h * HALF:(h + 1) * HALF],
                                start=True, stop=True)
            ins.then_inc(N[n]["sum"], 1)

        def x_ready(eng, n, kt):
            if n == 0:
                eng.wait_ge(x_in_sem[kt], 16)
            else:
                eng.wait_ge(N[n]["x"], kt + 1)

        def norm_act(act, n, kt):
            x_ready(act, n, kt)
            if n < 4:
                act.activation(XGh[:, kt, :], X[:, kt, :], ACT.Copy, scale=gcol(n, kt)).then_inc(N[n]["hi"], 1)
            wait(act, N[n]["used"], kt - 1)
            act.activation(sq[:, kt % 2, :], X[:, kt, :], ACT.Square).then_inc(N[n]["sq"], 1)

        def norm_lo(dve, n, kt):
            dve.wait_ge(N[n]["hi"], kt + 1)
            dve.scalar_tensor_tensor(out=XGl[:, kt, :], in0=X[:, kt, :], scalar=gcol(n, kt),
                                     in1=XGh[:, kt, :].bitcast(F32), op0=ALU.mult, op1=ALU.subtract
                                     ).then_inc(N[n]["lo"], 1)

        def norm_sum(pool, n, kt):
            pool.wait_ge(N[n]["sq"], kt + 1)
            if kt == 0:
                ins = pool.tensor_copy(acc[:, :], sq[:, 0, :])
            else:
                pool.wait_ge(N[n]["used"], kt)
                ins = pool.tensor_tensor(acc[:, :], acc[:, :], sq[:, kt % 2, :], ALU.add)
            ins.then_inc(N[n]["used"], 1)

        def norm_root(act, n):
            act.wait_ge(N[n]["sum"], 1)
            act.activation(sq[:, 0, :], slot(3), ACT.Sqrt, bias=epsb[:, 0:1], scale=1.0 / D).then_inc(N[n]["root"], 1)

        def norm_r(dve, n):
            dve.wait_ge(N[n]["root"], 1)
            dve.reciprocal(R[:, :], sq[:, 0, :]).then_inc(N[n]["r"], 1)
            dve.wait_ge(N[n]["r"], 1)

        def ffn_col(l, g, ht, kind, c):
            k = C_FFN + ((l * FT + ht) * 2 + kind) * 4 + c
            return par[:, k:k + 1] if isinstance(g, int) and g == 0 else par[:, bass.ds(g * 16 + k, 1)]

        def conv_col(ft, c):
            return par[:, bass.ds(ft * 3 + (C_CONV + c), 1)]

        def lagged(q, first, tail):
            return (not first or q >= 0) and (not tail or q < QT)

        def on(q, first, tail):
            return q % 2 == 0 and lagged(q, first, tail)

        def run_steps(eng, step, last):
            for ii in range(QT):
                step(0, ii, first=True)
            with eng.Fori(1, HEADS) as h:
                for ii in range(QT):
                    step(h, ii)
            for ii in range(QT, last + 1):
                step(HEADS - 1, ii, tail=True)

        LAST = GROUPS - 1

        def up_job(g, j, first):
            return j if first else 4 + (g - 1) * 12 + (0, 9, 10, 11)[j]

        def up_tile(g, j, first):
            return j if first else 4 + (g - 1) * 6 + (0, 3, 4, 5)[j]

        def down_job(g, m, final):
            return 4 + g * 12 + m + (0 if final else 1)

        def down_tile(g, d, final):
            return 4 + g * 6 + d + (0 if final else 1)


        @block.sync
        def _(sp):
            sp.dma_start(X[:, 0, :], x_in[0]).then_inc(x_in_sem[0], 16)
            sp.dma_start(par[:, :], params_in).then_inc(small_in, 16)
            sp.dma_start(con[:, :], consts_in).then_inc(small_in, 16)
            load_tile(sp, 0, 0)
            for kt in range(1, KT):
                sp.dma_start(X[:, kt, :], x_in[kt]).then_inc(x_in_sem[kt], 16)
            load_tile(sp, 1, 1)
            sp.dma_start(lams, lams_in.partition_broadcast(P)).then_inc(small_in, 16)
            sp.wait_ge(N[0]["lo"], KT)
            sp.wait_ge(N[0]["used"], KT)
            sp.dma_start(rot_a.bitcast(I32), positions.partition_broadcast(P)).then_inc(pos_in, 16)

            with sp.Fori(0, HEADS // 2) as pair:
                for a in range(2):
                    h = pair * 2 + a
                    n = pair * 6 + a * 3
                    load_tile(sp, n + 2, a % 2)
                    load_tile(sp, n + 3, (a + 1) % 2)
                    sp.wait_ge(q_out, h + 1)
                    sp.dma_start(q_dram[bass.ds(h, 1)].rearrange("a p n -> p (a n)"), q_res).then_inc(q_st, 16)
                    load_tile(sp, n + 4, a % 2)
                    sp.wait_ge(vt_out, h + 1)
                    sp.dma_start(v_dram[bass.ds(h, 1)].rearrange("a p n -> p (a n)"), vt_res).then_inc(v_st, 16)
                    sp.wait_ge(k_out, h + 1)
                    sp.dma_start(k_dram[bass.ds(h, 1)].rearrange("a p n -> p (a n)"), k_res).then_inc(k_st, 16)

            sp.wait_ge(q_st, 16 * HEADS)
            sp.wait_ge(k_st, 16 * HEADS)
            sp.wait_ge(v_st, 16 * HEADS)

            def load_head(h):
                for c in range(2):
                    for r, dram, made in ((c, k_dram, kl_made), (2 + c, q_dram, ql_made)):
                        wait(sp, made, 2 * h + c - 1)
                        for half in range(2):
                            sp.dma_start(X[half * HD:(half + 1) * HD, 4 + r, :],
                                         dram[bass.ds(h, 1), c * HD:(c + 1) * HD, :].rearrange("a p n -> p (a n)")
                                         ).then_inc(land_in[r], 16)
                wait(sp, vl_made, h)
                sp.dma_start(land[4], v_dram[bass.ds(h, 1)].rearrange("a p n -> p (a n)")).then_inc(land_in[4], 16)

            load_head(0)
            with sp.Fori(1, HEADS) as h:
                load_head(h)
            sp.wait_ge(kl_made, 2 * HEADS)
            sp.wait_ge(ql_made, 2 * HEADS)
            sp.dma_start(X[:, 4:8, :], x_in[4:8].rearrange("k p n -> p k n")).then_inc(x_again[1], 16)
            sp.wait_ge(t_done, HEADS * QT)
            sp.dma_start(X[:, 0:4, :], x_in[0:4].rearrange("k p n -> p k n")).then_inc(x_again[0], 16)
            with sp.Fori(T_WO // 2 + 1, T_END // 2) as pair:
                load_tile(sp, pair * 2, 0)
                load_tile(sp, pair * 2 + 1, 1)
            for kt in range(KT):
                sp.wait_ge(final_out, kt + 1)
                sp.dma_start(out[kt], X[:, kt, :]).then_inc(stored, 16)
            sp.wait_ge(stored, 16 * KT)


        @block.tensor
        def _(pe):
            def v_transpose(h):
                pe.wait_ge(v_out, h + 1)
                wait(pe, vt_out, h)
                for t in range(KT):
                    ins = pe.transpose(slot(3)[:, t * P:(t + 1) * P], v_res[:, t * P:(t + 1) * P], ident)
                ins.then_inc(vt_done, 1)

            def qkv_pair(pair, first):
                for a in range(2):
                    h = pair * 2 + a
                    n = pair * 6 + a * 3
                    wait(pe, v_out, h)
                    full_job(pe, n, a, 0, XGh, XGl, qkv_done,
                             (N[0]["hi"], N[0]["lo"]) if first and a == 0 else None)
                    if first and a == 0:
                        square_sum(pe, 0)
                    wait(pe, rot_read, 2 * h - 1)
                    full_job(pe, n + 1, (a + 1) % 2, 1, XGh, XGl, qkv_done)
                    if first and a == 0:
                        pe.wait_ge(N[0]["root"], 1)
                    v_transpose(h)
                    wait(pe, rot_read, 2 * h)
                    full_job(pe, n + 2, a, 2, XGh, XGl, qkv_done)

            pe.wait_ge(ones_set, 1)
            pe.wait_ge(small_in, 48)
            qkv_pair(0, True)
            with pe.Fori(1, HEADS // 2) as pair:
                qkv_pair(pair, False)

            def scores(h, i, q):
                for c in range(2):
                    if q == 0:
                        pe.wait_ge(kl_made, 2 * h + c + 1)
                        pe.wait_ge(ql_made, 2 * h + c + 1)
                    wait(pe, e_done, 2 * i + c - 1)
                    for half in range(2):
                        cols = slice(half * HALF, (half + 1) * HALF)
                        qs = Qs[c][:, q * P:(q + 1) * P]
                        pe.matmul(slot(c)[:, cols], qs, Kh[c][:, cols], start=True, stop=False)
                        ins = pe.matmul(slot(c)[:, cols], qs, Kl[c][:, cols], start=False, stop=True)
                    ins.then_inc(s_done, 1)

            def transposes(i, q):
                pe.wait_ge(a_done, i + 1)
                wait(pe, al_made, i)
                for t in range(KT):
                    ins = pe.transpose(slot(2)[:, t * P:(t + 1) * P], Pb[q % 2][1][:, t * P:(t + 1) * P], ident)
                ins.then_inc(t_done, 1)

            def values(h, u, quarter, part):
                b = quarter % 2
                if part == 0:
                    pe.wait_ge(al_made, 2 * u + 2)
                    wait(pe, o_sq, u)
                    if quarter == 0:
                        pe.wait_ge(vl_made, h + 1)
                for t in range(4 * part, 4 * part + 4):
                    c = slice(t * P, (t + 1) * P)
                    for w, m in ((0, Ah[b]), (0, Al[b]), (1, Ah[b])):
                        first, last = t == 0 and w == 0 and m is Ah[b], t == KT - 1 and w == 1
                        ins = pe.matmul(slot(3)[:, 0:2 * P], (Vh, Vl)[w][:, c], m[:, t, :], start=first, stop=last)
                if part == 1:
                    ins.then_inc(pv_done, 1)

            def subln_sum(u, quarter):
                pe.wait_ge(o_sq, u + 1)
                pe.wait_ge(dg_done, 2 * u + 2)
                wait(pe, ln_done, u)
                pe.matmul(slot(3)[:, HALF:HALF + 2 * P], ones[:, :], osq, start=True, stop=False)
                for t in range(2):
                    b = (2 * quarter + t) % 4
                    ins = pe.matmul(slot(3)[:, HALF + t * P:HALF + (t + 1) * P], ones[:, :],
                                    dg[:, b * P:(b + 1) * P], start=False, stop=t == 1)
                ins.then_inc(ss_done, 1)

            def step(h, ii, first=False, tail=False):
                i = h * QT + ii
                if not tail:
                    scores(h, i, ii)
                if on(ii - 5, first, tail):
                    subln_sum(h * 4 + (ii - 5) // 2, (ii - 5) // 2 % 4)
                if on(ii - 3, first, tail):
                    values(h, h * 4 + (ii - 3) // 2, (ii - 3) // 2 % 4, 0)
                if on(ii - 4, first, tail):
                    values(h, h * 4 + (ii - 4) // 2, (ii - 4) // 2 % 4, 1)
                if lagged(ii - 1, first, tail):
                    transposes(i - 1, (ii - 1) % QT)

            pe.wait_ge(v_out, HEADS)
            pe.wait_ge(rot_read, 2 * HEADS)
            pe.wait_ge(vt_out, HEADS)
            run_steps(pe, step, 12)

            def dense(d, base):
                def pair_of(pair):
                    for a in range(2):
                        n = pair * 2 + a
                        wait(pe, N[1 + 2 * d]["x"], n - 1)
                        full_job(pe, n + base, a, a, Yh, Yl, dense_done[d])
                pair_of(0)
                with pe.Fori(1, KT // 2) as pair:
                    pair_of(pair)

            pe.wait_ge(yh_made, 4 * HEADS)
            pe.wait_ge(yl_made, 4 * HEADS)
            dense(0, T_WO)

            def ffn(l, base, norm):
                f = F[l]

                def up(g, j, first=False):
                    if not first:
                        pe.wait_ge(f["free"], up_job(g, j, first) - 3)
                    full_job(pe, up_tile(g, j, first) + base, j % 2, j, XGh, XGl, f["done"],
                             (N[norm]["hi"], N[norm]["lo"]) if first and j == 0 else None)

                def down(g, final=False):
                    pe.wait_ge(f["hh"], 2 * g + 2)
                    pe.wait_ge(f["hl"], 2 * g + 2)
                    for m in range(KT):
                        d, s = m // 4, (m // 4 + (0 if final else 1)) % 2
                        if m % 4 == 0:
                            pe.wait_ge(w_lo, base + down_tile(g, d, final) + 1)
                        ps = (m + (0 if final else 1)) % 4
                        if final and m >= 4:
                            pe.wait_ge(N[norm + 1]["x"], m - 3)
                        else:
                            pe.wait_ge(f["free"], down_job(g, m, final) - 3)
                        for k in range(2):
                            c = slice((2 * (m % 4) + k) * P, (2 * (m % 4) + k + 1) * P)
                            ins = products(pe, slot(ps), Wh[:, s, c], Wl[:, s, c], Hh[:, k, :], Hl[:, k, :],
                                           k == 0, k == 1)
                        ins.then_inc(f["done"], 1)

                pe.wait_ge(N[norm]["x"], KT - 1)
                up(0, 0, True)
                square_sum(pe, norm)
                for j in (1, 2):
                    up(0, j, True)
                pe.wait_ge(N[norm]["root"], 1)
                up(0, 3, True)
                with pe.Fori(1, GROUPS) as g:
                    up(g, 0)
                    down(g - 1)
                    for j in (1, 2, 3):
                        up(g, j)
                down(LAST, True)

            ffn(0, T_FFN0, 1)

            def conv_pair(pair, first):
                for a in range(2):
                    for j in range(3):
                        n = pair * 6 + a * 3 + j
                        wait(pe, c_free, n - 2)
                        full_job(pe, n + T_CIN, (3 * a + j) % 2, j, XGh, XGl, c_done,
                                 (N[2]["hi"], N[2]["lo"]) if first and a == 0 and j == 0 else None)
                        if first and a == 0 and j == 0:
                            square_sum(pe, 2)

            pe.wait_ge(N[2]["x"], KT - 1)
            conv_pair(0, True)
            with pe.Fori(1, KT // 2) as pair:
                conv_pair(pair, False)
            pe.wait_ge(cyh, KT)
            pe.wait_ge(cyl, KT)
            dense(1, T_COUT)
            ffn(1, T_FFN1, 3)
            square_sum(pe, 4)


        @block.scalar
        def _(act):
            def w_hi_static(n, done=None, jobs=0):
                split_hi(act, n // 2, n % 2, done, jobs)

            act.wait_ge(small_in, 48)
            act.wait_ge(ones_set, 1)
            norm_act(act, 0, 0)
            w_hi_static(0)
            for kt in range(1, KT):
                norm_act(act, 0, kt)
            w_hi_static(1)

            def qkv_pair(pair, first):
                for a in range(2):
                    h = pair * 2 + a
                    for j in range(3):
                        c = 3 * a + j
                        split_hi(act, pair * 3 + (c + 2) // 2, c % 2, qkv_done, pair * 6 + c + 1)
                        if first and c == 0:
                            norm_root(act, 0)
                            act.wait_ge(tab, 10)
                            act.activation(sin_r, sin_r, ACT.Sin).then_inc(sin_done, 1)
                            act.activation(cos_r, cos_r, ACT.Sin).then_inc(sin_done, 1)
                        if j == 1:
                            act.wait_ge(vt_done, h + 1)
                            wait(act, v_st, h * 16)
                            act.activation(vt_res, slot(3), ACT.Copy).then_inc(vt_out, 1)

            qkv_pair(0, True)
            with act.Fori(1, HEADS // 2) as pair:
                qkv_pair(pair, False)

            act.preload_act_table_set("natural_log_exp_and_others")
            act.wait_ge(lam_sum, 4)
            act.activation(lam[:, 2:4], lam[:, 0:2], ACT.Exp).then_inc(lam_exp, 1)

            def head_start(h):
                for c in range(2):
                    wait(act, s_done, h * 2 * QT + c - 1)
                    act.wait_ge(land_in[c], 32 * (h + 1))
                    act.activation(Kh[c], land[c], ACT.Copy).then_inc(kh_made, 1)
                    act.wait_ge(land_in[2 + c], 32 * (h + 1))
                    act.activation(Qs[c], land[2 + c], ACT.Copy).then_inc(qh_made, 1)

            def step(h, ii, first=False, tail=False):
                i = h * QT + ii
                if not tail:
                    if ii == 0:
                        head_start(h)
                    for c in range(2):
                        act.wait_ge(nb_done, 2 * i + c + 1)
                        wait(act, t_done, i - 1)
                        act.activation(Pb[ii % 2][c], slot(c), ACT.Exp, bias=nb[:, 2 * (ii % 2) + c:2 * (ii % 2) + c + 1],
                                       scale=SCALE, accum_out=rsum[:, c, ii:ii + 1]).then_inc(e_done, 1)
                if on(ii - 4, first, tail):
                    u = h * 4 + (ii - 4) // 2
                    act.wait_ge(pv_done, u + 1)
                    wait(act, o_scaled, u)
                    act.activation(osb, slot(3)[:, 0:2 * P], ACT.Copy).then_inc(o_copied, 1)
                    wait(act, ss_done, u)
                    act.activation(osq, slot(3)[:, 0:2 * P], ACT.Square).then_inc(o_sq, 1)
                if on(ii - 5, first, tail):
                    u = h * 4 + (ii - 5) // 2
                    act.wait_ge(ss_done, u + 1)
                    act.activation(z, slot(3)[:, HALF:HALF + 2 * P], ACT.Ln, scale=1.0 / VD).then_inc(ln_done, 1)
                    act.wait_ge(ln_done, u + 1)
                    act.activation(z, z, ACT.Exp, scale=-0.5).then_inc(z_done, 1)
                if lagged(ii - 1, first, tail):
                    q = (ii - 1) % QT
                    act.wait_ge(t_done, i)
                    if q % 2 == 0:
                        wait(act, pv_done, h * 4 + (ii - 1) // 2 - 1)
                    act.activation(Ah[q // 2 % 2][:, :, q % 2 * P:(q % 2 + 1) * P],
                                   slot(2).rearrange("p (t n) -> p t n", n=P), ACT.Copy).then_inc(ah_made, 1)
                if on(ii - 7, first, tail):
                    u, uq = h * 4 + (ii - 7) // 2, (ii - 7) // 2
                    act.wait_ge(o_scaled, u + 1)
                    act.activation(Yh[:, bass.ds(h + uq // 4, 1), uq % 4 * 2 * P:(uq % 4 + 1) * 2 * P], ot3, ACT.Copy,
                                   scale=lam[:, 5:6]).then_inc(yh_made, 1)
                if not tail and ii == 2:
                    wait(act, pv_done, 4 * h)
                    act.wait_ge(land_in[4], 16 * (h + 1))
                    act.activation(Vh, land[4], ACT.Copy).then_inc(vh_made, 1)

            act.wait_ge(lam_done, 2)
            run_steps(act, step, 14)

            def dense(d, base, norm):
                for kt in range(KT):
                    w_hi_static(base + kt + 2, dense_done[d], kt + 1)
                    norm_act(act, norm, kt)

            dense(0, T_WO, 1)

            def ffn(l, base, norm):
                f = F[l]

                def split_next(t_half, s, jobs):
                    split_hi(act, base // 2 + t_half, s, f["done"], jobs)

                def up(g, j, first):
                    t_off = j if first else (0, 3, 4, 5)[j]
                    t_half = (t_off + 2) // 2 if first else 2 + (g - 1) * 3 + (t_off + 2) // 2
                    split_next(t_half, t_off % 2, up_job(g, j, first) + 1)
                    if first and j == 0:
                        norm_root(act, norm)
                    kind, ht = j % 2, j // 2
                    act.wait_ge(f["free"], up_job(g, j, first) + 1)
                    if kind == 0:
                        wait(act, f["h"], 2 * g + ht)
                        dst = Tg[:, :]
                    else:
                        wait(act, f["hl"], 2 * g + ht - 1)
                        dst = Tv[:, ht, :]
                    act.activation(dst, raws[kind][:, 1:S + 1], ACT.Identity, bias=ffn_col(l, g, ht, kind, 3),
                                   scale=ffn_col(l, g, ht, kind, 1)).then_inc(f["mid"], 1)
                    act.wait_ge(f["conv"], 4 * g + j + 1) if kind == 0 else None
                    if kind == 0:
                        act.activation(Tg[:, :], Tg[:, :], ACT.Silu).then_inc(f["silu"], 1)
                    else:
                        act.wait_ge(f["h"], 2 * g + ht + 1)
                        act.activation(Hh[:, ht, :], Tv[:, ht, :], ACT.Copy).then_inc(f["hh"], 1)

                for j in range(4):
                    up(0, j, True)
                with act.Fori(1, GROUPS) as g:
                    up(g, 0, False)
                    for d in range(2):
                        split_next(2 + (g - 1) * 3 + (3 + d) // 2, (1 + d) % 2, down_job(g - 1, 4 * d + 3, False) + 1)
                    for j in (1, 2, 3):
                        up(g, j, False)
                for m in range(KT):
                    if m % 4 == 3 and norm < 3:
                        w_hi_static(base + down_tile(LAST, m // 4, True) + 2, f["done"], down_job(LAST, m, True) + 1)
                    norm_act(act, norm + 1, m)

            ffn(0, T_FFN0, 1)

            def conv_pair(pair, first):
                for a in range(2):
                    ft = pair * 2 + a
                    for j in range(3):
                        c = 3 * a + j
                        split_hi(act, T_CIN // 2 + pair * 3 + (c + 2) // 2, c % 2, c_done, pair * 6 + c + 1)
                        if first and c == 0:
                            norm_root(act, 2)
                        if j == 1:
                            act.wait_ge(cu_made, ft + 1)
                            act.activation(sq[:, 1, :], cu[:, 1:S + 1], ACT.Copy, scale=conv_col(ft, 1)).then_inc(ct_mid, 1)
                    act.wait_ge(cy_made, ft + 1)
                    act.activation(Yh[:, bass.ds(ft, 1), :], sq[:, 0:1, :], ACT.Copy).then_inc(cyh, 1)

            conv_pair(0, True)
            with act.Fori(1, KT // 2) as pair:
                conv_pair(pair, False)
            dense(1, T_COUT, 3)
            ffn(1, T_FFN1, 3)
            norm_root(act, 4)


        @block.vector
        def _(dve):
            dve.memset(epsb[:, :], EPS)
            dve.memset(ones[:, :], 1.0).then_inc(ones_set, 1)
            dve.wait_ge(small_in, 48)
            for kt in range(KT):
                norm_lo(dve, 0, kt)

            def tabled(count, ins):
                ins.then_inc(tab, 1)
                dve.wait_ge(tab, count)

            dve.wait_ge(pos_in, 16)
            ang, k_ = sin_r, cos_r
            tabled(1, dve.tensor_scalar(ang, rot_a.bitcast(I32), con[:, C_FREQ:C_FREQ + 1], None, ALU.mult))
            tabled(2, dve.tensor_scalar(k_, ang, 1.0 / (2.0 * np.pi), MAGIC, ALU.mult, ALU.add))
            tabled(3, dve.tensor_scalar(k_, k_, -MAGIC, None, ALU.add))
            for t in range(3):
                tabled(4 + t, dve.scalar_tensor_tensor(out=ang, in0=k_, scalar=-TWO_PI[t], in1=ang,
                                                       op0=ALU.mult, op1=ALU.add))
            tabled(7, dve.tensor_scalar(k_, ang, float(np.pi / 2), -2.0 * np.pi, ALU.is_gt, ALU.mult))
            tabled(8, dve.scalar_tensor_tensor(out=k_, in0=ang, scalar=float(np.pi / 2), in1=k_,
                                               op0=ALU.add, op1=ALU.add))
            tabled(9, dve.tensor_scalar(k_, k_, PI_IN, -PI_IN, ALU.min, ALU.max))
            tabled(10, dve.tensor_scalar(ang, ang, PI_IN, -PI_IN, ALU.min, ALU.max))
            norm_r(dve, 0)
            dve.wait_ge(sin_done, 2)
            tabled(11, dve.tensor_tensor(cos_r, cos_r, R[:, :], ALU.mult))
            tabled(12, dve.scalar_tensor_tensor(out=sin_r, in0=sin_r, scalar=con[:, C_SIGN:C_SIGN + 1], in1=R[:, :],
                                                op0=ALU.mult, op1=ALU.mult))

            def rotate(n_done, n_rot, ps_slot, res, out_sem, h, st_sem, before, count):
                dve.wait_ge(qkv_done, n_done)
                wait(dve, before, count)
                dve.tensor_tensor(rot_a, slot(ps_slot), cos_r, ALU.mult).then_inc(rot_sum, 1)
                for q in range(4):
                    o, i = slice(32 * q, 32 * q + 32), slice(32 * (q ^ 1), 32 * (q ^ 1) + 32)
                    ins = dve.tensor_tensor(rot_b[o], slot(ps_slot)[i], sin_r[o], ALU.mult)
                ins.then_inc(rot_read, 1)
                dve.wait_ge(rot_sum, n_rot)
                dve.wait_ge(rot_read, n_rot)
                wait(dve, st_sem, h * 16)
                dve.tensor_tensor(res, rot_a, rot_b, ALU.add).then_inc(out_sem, 1)

            def qkv_head(h):
                dve.wait_ge(qkv_done, 3 * h + 1)
                wait(dve, vt_done, h)
                dve.tensor_tensor(v_res, slot(0), R[:, :], ALU.mult).then_inc(v_out, 1)
                rotate(3 * h + 2, 2 * h + 1, 1, q_res, q_out, h, q_st, k_out, h)
                rotate(3 * h + 3, 2 * h + 2, 2, k_res, k_out, h, k_st, q_out, h + 1)

            qkv_head(0)
            with dve.Fori(1, HEADS) as h:
                qkv_head(h)

            for c in range(2):
                pr = cu[:, 4 * HD + c * HD:4 * HD + (c + 1) * HD]
                dve.tensor_tensor(pr, lams[:, 2 * c * HD:(2 * c + 1) * HD], lams[:, (2 * c + 1) * HD:(2 * c + 2) * HD],
                                  ALU.mult).then_inc(lam_sum, 1)
                dve.wait_ge(lam_sum, 2 * c + 1)
                dve.reduce_sum(lam[:, c:c + 1], pr, axis=AX_X).then_inc(lam_sum, 1)
            dve.tensor_scalar(lam[:, 5:6], par[:, C_SUBG:C_SUBG + 1], 1.0 - LAMBDA_INIT, None, ALU.mult
                              ).then_inc(lam_done, 1)
            dve.wait_ge(lam_exp, 1)
            dve.scalar_tensor_tensor(out=lam[:, 4:5], in0=lam[:, 3:4], scalar=-LAMBDA_INIT, in1=lam[:, 2:3],
                                     op0=ALU.add, op1=ALU.subtract).then_inc(lam_done, 1)
            dve.wait_ge(lam_done, 2)

            def step(h, ii, first=False, tail=False):
                i = h * QT + ii
                if not tail:
                    if ii == 0:
                        for c in range(2):
                            dve.wait_ge(qh_made, 2 * h + c + 1)
                            up = slice(HD, P)
                            dve.tensor_tensor(Qs[c][up], land[2 + c][up], Qs[c][up].bitcast(F32), ALU.subtract
                                              ).then_inc(ql_made, 1)
                    for c in range(2):
                        b = 2 * (ii % 2) + c
                        dve.wait_ge(s_done, 2 * i + c + 1)
                        dve.reduce_max(mx[:, b:b + 1], slot(c), axis=AX_X).then_inc(mx_done, 1)
                        dve.wait_ge(mx_done, 2 * i + c + 1)
                        dve.tensor_scalar(nb[:, b:b + 1], mx[:, b:b + 1], -SCALE, None, ALU.mult).then_inc(nb_done, 1)
                if on(ii - 8, first, tail):
                    u, uq = h * 4 + (ii - 8) // 2, (ii - 8) // 2
                    dve.wait_ge(yh_made, u + 1)
                    dst = (bass.ds(h + uq // 4, 1), slice(uq % 4 * 2 * P, (uq % 4 + 1) * 2 * P))
                    dve.scalar_tensor_tensor(out=Yl[:, dst[0], dst[1]], in0=ot3, scalar=lam[:, 5:6],
                                             in1=Yh[:, dst[0], dst[1]].bitcast(F32), op0=ALU.mult, op1=ALU.subtract
                                             ).then_inc(yl_made, 1)
                if on(ii - 6, first, tail):
                    u = h * 4 + (ii - 6) // 2
                    dve.wait_ge(z_done, u + 1)
                    wait(dve, yl_made, u)
                    dve.tensor_tensor(ot, osb, z, ALU.mult).then_inc(o_scaled, 1)
                if not tail and ii == 3:
                    dve.wait_ge(vh_made, h + 1)
                    dve.tensor_tensor(Vl, land[4], Vh.bitcast(F32), ALU.subtract).then_inc(vl_made, 1)
                if lagged(ii - 2, first, tail):
                    q = (ii - 2) % QT
                    cols = slice(q % 2 * P, (q % 2 + 1) * P)
                    dve.wait_ge(ah_made, i - 1)
                    dve.tensor_tensor(Al[q // 2 % 2][:, :, cols], slot(2).rearrange("p (t n) -> p t n", n=P),
                                      Ah[q // 2 % 2][:, :, cols].bitcast(F32), ALU.subtract).then_inc(al_made, 1)
                if lagged(ii - 1, first, tail):
                    q = (ii - 1) % QT
                    dve.wait_ge(e_done, 2 * i)
                    dve.reciprocal(coef[:, 0:1], rsum[:, 1, q:q + 1]).then_inc(co_done, 1)
                    dve.wait_ge(co_done, 2 * i - 1)
                    dve.scalar_tensor_tensor(out=coef[:, 1:2], in0=rsum[:, 0, q:q + 1], scalar=lam[:, 4:5],
                                             in1=coef[:, 0:1], op0=ALU.mult, op1=ALU.mult).then_inc(co_done, 1)
                    dve.wait_ge(co_done, 2 * i)
                    dve.scalar_tensor_tensor(out=Pb[q % 2][1], in0=Pb[q % 2][1], scalar=coef[:, 1:2],
                                             in1=Pb[q % 2][0], op0=ALU.mult, op1=ALU.add).then_inc(a_done, 1)

            run_steps(dve, step, 15)

            def add_and_norm(kt, ps_slot, done, jobs, norm):
                dve.wait_ge(done, jobs)
                dve.tensor_tensor(X[:, kt, :], slot(ps_slot), X[:, kt, :], ALU.add).then_inc(N[norm]["x"], 1)
                if norm < 4 and kt:
                    norm_lo(dve, norm, kt - 1)

            dve.wait_ge(x_again[0], 16)
            dve.wait_ge(x_again[1], 16)
            for kt in range(KT):
                add_and_norm(kt, kt % 2, dense_done[0], kt + 1, 1)
            norm_lo(dve, 1, KT - 1)

            def ffn(l, norm):
                f = F[l]
                for t in (rawg, rawv):
                    dve.memset(t[:, 0:1], 0.0)
                    ins = dve.memset(t[:, S + 1:S + 2], 0.0)
                ins.then_inc(f["pad"], 1)
                dve.wait_ge(f["pad"], 1)
                norm_r(dve, norm)

                def up(g, j, first):
                    kind, ht = j % 2, j // 2
                    dve.wait_ge(f["done"], up_job(g, j, first) + 1)
                    raw = raws[kind]
                    dve.tensor_tensor(raw[:, 1:S + 1], slot(j), R[:, :], ALU.mult).then_inc(f["free"], 1)
                    T = Tg[:, :] if kind == 0 else Tv[:, ht, :]
                    dve.wait_ge(f["mid"], 4 * g + j + 1)
                    dve.scalar_tensor_tensor(out=T, in0=raw[:, 0:S], scalar=ffn_col(l, g, ht, kind, 0), in1=T,
                                             op0=ALU.mult, op1=ALU.add).then_inc(f["tap"], 1)
                    dve.wait_ge(f["tap"], 4 * g + j + 1)
                    dve.scalar_tensor_tensor(out=T, in0=raw[:, 2:S + 2], scalar=ffn_col(l, g, ht, kind, 2), in1=T,
                                             op0=ALU.mult, op1=ALU.add).then_inc(f["conv"], 1)
                    if kind == 1:
                        dve.wait_ge(f["conv"], 4 * g + j + 1)
                        dve.wait_ge(f["silu"], 2 * g + ht + 1)
                        dve.tensor_tensor(T, Tg[:, :], T, ALU.mult).then_inc(f["h"], 1)
                        dve.wait_ge(f["hh"], 2 * g + ht + 1)
                        dve.tensor_tensor(Hl[:, ht, :], T, Hh[:, ht, :].bitcast(F32), ALU.subtract
                                          ).then_inc(f["hl"], 1)

                for j in range(4):
                    up(0, j, True)
                with dve.Fori(1, GROUPS) as g:
                    up(g, 0, False)
                    for m in range(KT):
                        dve.wait_ge(f["done"], down_job(g - 1, m, False) + 1)
                        dve.tensor_tensor(X[:, m, :], slot((m + 1) % 4), X[:, m, :], ALU.add).then_inc(f["free"], 1)
                    for j in (1, 2, 3):
                        up(g, j, False)
                for m in range(KT):
                    add_and_norm(m, m % 4, f["done"], down_job(LAST, m, True) + 1, norm + 1)
                if norm < 3:
                    norm_lo(dve, norm + 1, KT - 1)

            ffn(0, 1)

            dve.memset(cu[:, 0:1], 0.0)
            dve.memset(cu[:, S + 1:S + 2], 0.0).then_inc(c_pad, 1)
            dve.wait_ge(c_pad, 1)
            norm_r(dve, 2)

            def conv_tile(ft):
                n = ft * 3
                c_t, u_t, T = acc[:, :], sq[:, 0, :], sq[:, 1, :]
                dve.wait_ge(c_done, n + 1)
                dve.tensor_tensor(c_t, slot(0), R[:, :], ALU.mult).then_inc(c_free, 1)
                dve.wait_ge(c_done, n + 2)
                wait(dve, cyl, ft)
                dve.tensor_tensor(u_t, slot(1), R[:, :], ALU.mult).then_inc(c_free, 1)
                dve.wait_ge(c_free, n + 2)
                dve.tensor_tensor(cu[:, 1:S + 1], c_t, u_t, ALU.mult).then_inc(cu_made, 1)
                dve.wait_ge(ct_mid, ft + 1)
                for e, (off, tap) in enumerate(((0, 0), (2, 2))):
                    dve.scalar_tensor_tensor(out=T, in0=cu[:, off:off + S], scalar=conv_col(ft, tap), in1=T,
                                             op0=ALU.mult, op1=ALU.add).then_inc(ct_made, 1)
                    dve.wait_ge(ct_made, 2 * ft + e + 1)
                dve.wait_ge(c_done, n + 3)
                dve.tensor_tensor(c_t, slot(2), R[:, :], ALU.mult).then_inc(c_free, 1)
                dve.wait_ge(c_free, n + 3)
                dve.tensor_tensor(u_t, T, c_t, ALU.mult).then_inc(cy_made, 1)
                dve.wait_ge(cyh, ft + 1)
                dve.tensor_tensor(Yl[:, bass.ds(ft, 1), :], sq[:, 0:1, :], Yh[:, bass.ds(ft, 1), :].bitcast(F32),
                                  ALU.subtract).then_inc(cyl, 1)

            conv_tile(0)
            with dve.Fori(1, KT) as ft:
                conv_tile(ft)
            for kt in range(KT):
                add_and_norm(kt, kt % 2, dense_done[1], kt + 1, 3)
            norm_lo(dve, 3, KT - 1)
            ffn(1, 3)
            norm_r(dve, 4)
            for kt in range(KT):
                dve.scalar_tensor_tensor(out=X[:, kt, :], in0=X[:, kt, :], scalar=gcol(4, kt), in1=R[:, :],
                                         op0=ALU.mult, op1=ALU.mult).then_inc(final_out, 1)


        @block.gpsimd
        def _(pool):
            norm_sum(pool, 0, 0)
            split_lo(pool, 0, 0)
            for kt in range(1, KT):
                norm_sum(pool, 0, kt)
            split_lo(pool, 1, 1)
            with pool.Fori(1, T_WO // 2 + 1) as pair:
                for a in range(2):
                    split_lo(pool, pair * 2 + a, a)

            pool.wait_ge(lam_done, 2)

            def step(h, ii, first=False, tail=False):
                i = h * QT + ii
                if not tail and ii == 0:
                    for c in range(2):
                        pool.wait_ge(kh_made, 2 * h + c + 1)
                        pool.tensor_tensor(Kl[c], land[c], Kh[c].bitcast(F32), ALU.subtract).then_inc(kl_made, 1)
                if lagged(ii - 1, first, tail):
                    q = (ii - 1) % QT
                    pool.wait_ge(e_done, 2 * i - 1)
                    wait(pool, dg_done, i - 1)
                    pool.tensor_tensor(coef[:, 2:3], rsum[:, 0, q:q + 1], rsum[:, 0, q:q + 1], ALU.mult
                                       ).then_inc(s0sq_done, 1)
                    pool.wait_ge(s0sq_done, i)
                    wait(pool, ss_done, h * 4 + (ii - 5) // 2 + 1)
                    pool.tensor_tensor(dg[:, q % 4 * P:(q % 4 + 1) * P], con[:, C_EPSI:C_EPSI + P],
                                       coef[:, 2:3].to_broadcast([P, P]), ALU.mult).then_inc(dg_done, 1)

            run_steps(pool, step, 9)

            def dense(base, norm):
                for kt in range(KT):
                    split_lo(pool, base + kt + 2, kt % 2)
                    norm_sum(pool, norm, kt)

            def ffn(base, norm):
                with pool.Fori((base + 2) // 2, (base + 2 * FT + 2 * GROUPS) // 2) as pair:
                    for a in range(2):
                        split_lo(pool, pair * 2 + a, a)
                for m in range(KT):
                    if m % 4 == 3 and norm < 3:
                        n = base + down_tile(LAST, m // 4, True) + 2
                        split_lo(pool, n, n % 2)
                    norm_sum(pool, norm + 1, m)

            dense(T_WO, 1)
            ffn(T_FFN0, 1)
            with pool.Fori((T_CIN + 2) // 2, (T_COUT + 2) // 2) as pair:
                for a in range(2):
                    split_lo(pool, pair * 2 + a, a)
            dense(T_COUT, 3)
            ffn(T_FFN1, 3)


def _up_tiles(w):
    n = w.shape[1] // P
    return w.reshape(KT, P, n, P).transpose(2, 1, 0, 3).reshape(n, P, D)


def _down_tiles(w):
    return w.reshape(GROUPS, 2, P, 2, 4, P).transpose(0, 3, 2, 4, 1, 5).reshape(GROUPS, 2, P, D)


def _ffn_tiles(w_up, w_down):
    up, down = _up_tiles(w_up), _down_tiles(w_down)
    gate, val = up[:FT], up[FT:]
    order = [gate[0], val[0], gate[1], val[1]]
    for g in range(1, GROUPS):
        order += [gate[2 * g], down[g - 1, 0], down[g - 1, 1], val[2 * g], gate[2 * g + 1], val[2 * g + 1]]
    return np.stack(order + [down[GROUPS - 1, 0], down[GROUPS - 1, 1]])


def kernel(x, positions, attn_norm_g, attn_w_qkv, attn_lambda_q1, attn_lambda_k1, attn_lambda_q2, attn_lambda_k2,
           attn_subln_g, attn_w_o, conv_norm_g, conv_w_in, conv_w, conv_w_out, ffn_norm_g, ffn_w_up, ffn_conv_w,
           ffn_conv_b, ffn_w_down, final_norm_g):
    import concourse.bacc as bacc
    from concourse.bass_utils import run_bass_kernel_spmd

    a = {k: np.asarray(v) for k, v in locals().items() if k not in ("bacc", "run_bass_kernel_spmd")}
    qkv = _up_tiles(a["attn_w_qkv"][0]).reshape(3, HEADS, P, D)
    qkv = np.stack([qkv[2], qkv[0], qkv[1]], axis=1).reshape(3 * HEADS, P, D)
    cin = _up_tiles(a["conv_w_in"][0]).reshape(3, KT, P, D)
    cin = np.stack([cin[1], cin[2], cin[0]], axis=1).reshape(3 * KT, P, D)
    weights = np.concatenate([
        qkv, _up_tiles(a["attn_w_o"][0]), _ffn_tiles(a["ffn_w_up"][0], a["ffn_w_down"][0]),
        cin, _up_tiles(a["conv_w_out"][0]), _ffn_tiles(a["ffn_w_up"][1], a["ffn_w_down"][1])])
    norms = np.stack([a["attn_norm_g"][0], a["ffn_norm_g"][0], a["conv_norm_g"][0], a["ffn_norm_g"][1],
                      a["final_norm_g"]]).reshape(5 * KT, P)
    taps = np.concatenate([a["ffn_conv_w"], a["ffn_conv_b"][:, None]], axis=1)
    taps = taps.reshape(2, 4, 2, FT, P).transpose(0, 3, 2, 1, 4).reshape(2 * FT * 2 * 4, P)
    conv = a["conv_w"][0].reshape(3, KT, P).transpose(1, 0, 2).reshape(KT * 3, P)
    params = np.concatenate([norms, taps, conv, a["attn_subln_g"]]).T
    lams = np.concatenate([a["attn_lambda_q1"][0], a["attn_lambda_k1"][0], a["attn_lambda_q2"][0],
                           a["attn_lambda_k2"][0]])
    freq = (np.float32(THETA) ** (-np.arange(0, HD, 2, dtype=np.float32) / np.float32(HD))).astype(np.float32)
    sign = np.repeat(np.array([-1, 1, -1, 1], np.float32), 32)
    consts = np.concatenate([np.tile(freq, 4)[:, None], sign[:, None], np.eye(P, dtype=np.float32),
                             np.eye(P, dtype=np.float32) * np.float32(VD * EPS)], axis=1)
    ins = {
        "x_tiles": a["x"][0].T.reshape(KT, P, S), "positions": a["positions"][0], "weights": weights,
        "params": params, "consts": consts, "lams": lams,
    }
    nc = bacc.Bacc("TRN2", target_bir_lowering=False, num_devices=1)
    arrays, args = {}, []
    for name, v in ins.items():
        arrays[name] = np.ascontiguousarray(v)
        args.append(nc.dram_tensor(name, v.shape, mybir.dt.from_np(v.dtype), kind="ExternalInput").ap())
    args.append(nc.dram_tensor("y_tiles", (KT, P, S), F32, kind="ExternalOutput").ap())
    build(nc, *args)
    r = run_bass_kernel_spmd(nc, [arrays], core_ids=[0])
    return np.ascontiguousarray(r.results[0]["y_tiles"].reshape(D, S).T[None])
```

```python
from contextlib import ExitStack

import numpy as np

import concourse.bass as bass
from concourse import mybir

F32 = mybir.dt.float32
F32R = mybir.dt.float32r
I32 = mybir.dt.int32
ALU = mybir.AluOpType
ACT = mybir.ActivationFunctionType
AX_X = mybir.AxisListType.X

P = 128
D = 1024
S = 1024
KT = D // P
HALF = 512
DFF = 2816
FT = DFF // P
GROUPS = FT // 2
HEADS = 8
HD = 64
VD = 2 * HD
QT = S // P
EPS = 1e-5
THETA = 10000.0
LAMBDA_INIT = 0.2
SCALE = HD ** -0.5
MAGIC = 1.5 * 2.0 ** 23
TWO_PI = (6.28125, 0.0019350051879882812, 3.01991598196e-07)
PI_IN = 3.1415925

C_NORM = 0
C_FFN = C_NORM + 5 * KT
C_CONV = C_FFN + 2 * FT * 2 * 4
C_SUBG = C_CONV + KT * 3
N_PARAM = C_SUBG + 1

C_FREQ, C_SIGN, C_IDENT, C_EPSI = 0, 1, 2, 2 + P
N_CONST = 2 + 2 * P

T_QKV = 0
T_WO = T_QKV + 3 * HEADS
T_FFN0 = T_WO + KT
T_CIN = T_FFN0 + 2 * FT + 2 * GROUPS
T_COUT = T_CIN + 3 * KT
T_FFN1 = T_COUT + KT
T_END = T_FFN1 + 2 * FT + 2 * GROUPS


def wait(eng, sem, value):
    if isinstance(value, int) and value <= 0:
        return
    eng.wait_ge(sem, value)


def build(nc, x_in, positions, weights, params_in, consts_in, lams_in, out):
    ctx = ExitStack()
    with ctx:
        def sb(name, shape, dt=F32, stack=ctx):
            return stack.enter_context(nc.sbuf_tensor(name, shape, dt))

        def sem(name):
            return ctx.enter_context(nc.semaphore(name))

        q_dram = nc.dram_tensor("q_scratch", (HEADS, P, S), F32, kind="Internal").ap()
        k_dram = nc.dram_tensor("k_scratch", (HEADS, P, S), F32, kind="Internal").ap()
        v_dram = nc.dram_tensor("v_scratch", (HEADS, P, S), F32, kind="Internal").ap()

        X = sb("X", [P, KT, S])
        XGh = sb("XGh", [P, KT, S], F32R)
        XGl = sb("XGl", [P, KT, S], F32R)
        Wraw = sb("Wraw", [P, 2, 1024])
        Wh = sb("Wh", [P, 2, 1024], F32R)
        Wl = sb("Wl", [P, 2, 1024], F32R)
        R = sb("R", [P, S])
        acc = sb("acc", [P, S])
        sq = sb("sq", [P, 2, S])
        cu = sb("cu", [P, S + 2])
        par = sb("par", [P, N_PARAM])
        con = sb("con", [P, N_CONST])
        ones = sb("ones", [P, P])
        lam = sb("lam", [P, 8])
        nb = sb("nb", [P, 4])
        rsum = sb("rsum", [P, 2, QT])
        coef = sb("coef", [P, 4])
        epsb = sb("epsb", [P, 1])
        with ExitStack() as one:
            Yh = sb("Yh", [P, KT, S], F32R, one)
            Yl = sb("Yl", [P, KT, S], F32R, one)
        with ExitStack() as two:
            Hh = sb("Hh", [P, 2, S], F32R, two)
            Hl = sb("Hl", [P, 2, S], F32R, two)
            rawg = sb("rawg", [P, S + 2], F32, two)
            rawv = sb("rawv", [P, S + 2], F32, two)
            Tg = sb("Tg", [P, S], F32, two)
            Tv = sb("Tv", [P, 2, S], F32, two)
        PS = ctx.enter_context(nc.psum_tensor("PS", [P, 4096], F32))
        ident = con[:, C_IDENT:C_IDENT + P]
        raws = (rawg, rawv)
        cos_r, sin_r, rot_a, rot_b, q_res, k_res, v_res, vt_res = (X[:, t, :] for t in range(KT))
        P0 = [X[:, 0, :], X[:, 1, :]]
        P1 = [X[:, 2, :], X[:, 3, :], R[:, :], sq[:, 1, :]]
        land = [X[:, 4 + r, :] for r in range(4)] + [acc[:, :]]
        Kh = [[Yh[:, 6 + c, :] for c in range(2)], [XGh[:, c, :] for c in range(2)]]
        Kl = [[Yl[:, 6 + c, :] for c in range(2)], [XGh[:, 2 + c, :] for c in range(2)]]
        Q_later, Q_first = [XGh[:, 4, :], XGh[:, 5, :]], [Yh[:, 5, :], Yl[:, 5, :]]
        V = [XGh[:, 6, :], XGh[:, 7, :]]
        land_first = [sq[:, 0, :], sq[:, 1, :]]

        def is_first(h):
            return isinstance(h, int) and h == 0

        def is_last(h):
            return isinstance(h, int) and h == HEADS - 1

        def Q_of(h):
            return Q_first if is_first(h) else Q_later
        Ah = [XGl[:, 2 * b:2 * b + 2, :].rearrange("p a (t n) -> p (a t) n", n=2 * P) for b in range(2)]
        Al = [XGl[:, 4 + 2 * b:6 + 2 * b, :].rearrange("p a (t n) -> p (a t) n", n=2 * P) for b in range(2)]
        osq, osb, z, ot = (sq[:, 0, t * 2 * P:(t + 1) * 2 * P] for t in range(4))
        ot3 = sq[:, 0:1, 6 * P:8 * P]
        dg = cu[:, 0:QT * P]
        lams = cu[:, 0:4 * HD]

        def slot(s):
            return PS[:, s * 1024:(s + 1) * 1024]

        def gcol(norm, kt):
            return par[:, C_NORM + norm * KT + kt:C_NORM + norm * KT + kt + 1]

        w_in = [sem("w_in0"), sem("w_in1")]
        w_hi, w_lo = sem("w_hi"), sem("w_lo")
        x_in_sem = [sem(f"x_in{k}") for k in range(KT)]
        x_again = [sem(f"x_again{k}") for k in range(2)]
        first_in = [sem("k_first"), sem("q_first"), sem("v_first")]
        small_in, ones_set, pos_in = sem("small_in"), sem("ones_set"), sem("pos_in")
        lam_ch = sem("lam_ch")
        stored = sem("stored")
        N = [dict(x=sem(f"n{n}_x_final"), hi=sem(f"n{n}_hi"), lo=sem(f"n{n}_lo"), sq=sem(f"n{n}_sq"),
                  used=sem(f"n{n}_sq_used"), sum=sem(f"n{n}_sum"), read=sem(f"n{n}_sum_read"), r=sem(f"n{n}_r"))
             for n in range(5)]
        final_out = sem("final_out")
        qkv_done, v_out, rot_read, rot_sum = sem("qkv_done"), sem("v_out"), sem("rot_read"), sem("rot_sum")
        vt_done, vt_out, q_out, k_out = sem("vt_done"), sem("vt_out"), sem("q_out"), sem("k_out")
        q_st, k_st, v_st = sem("q_stored"), sem("k_stored"), sem("v_stored")
        tab, sin_done = sem("rotary_tables"), sem("sin_done")
        lam_sum, lam_exp, lam_done = sem("lam_sum"), sem("lam_exp"), sem("lam_done")
        land_in = [sem(f"landed{r}") for r in range(5)]
        kh_made, kl_made, qh_made, ql_made = sem("kh_made"), sem("kl_made"), sem("qh_made"), sem("ql_made")
        vh_made, vl_made = sem("vh_made"), sem("vl_made")
        s_done, nb_done, e_done = sem("s_done"), sem("nb_done"), sem("e_done")
        inv_done, co_done, a_done, t_done = sem("inverse_done"), sem("coef_done"), sem("a_done"), sem("t_done")
        ah_made, al_made = sem("ah_made"), sem("al_made")
        s0sq_done, dg_done = sem("s0sq_done"), sem("dg_done")
        pv_half = sem("pv_half")
        pv_done, o_copied, o_sq, ss_done = sem("pv_done"), sem("o_copied"), sem("o_squared"), sem("ss_done")
        ln_done, z_done, o_scaled = sem("ln_done"), sem("z_done"), sem("o_scaled")
        yh_made, yl_made = sem("yh_made"), sem("yl_made")
        dense_done = [sem("dense0_done"), sem("dense1_done")]
        c_done, c_free, cu_made, ct_mid, ct_made = (sem("conv_mm_done"), sem("conv_mm_free"), sem("cu_made"),
                                                    sem("ct_mid"), sem("ct_made"))
        cy_made, cyh, cyl, c_pad = sem("cy_made"), sem("cyh_made"), sem("cyl_made"), sem("conv_pad")
        F = [{k: sem(f"f{l}_{k}") for k in ("done", "free", "mid", "tap", "conv", "silu", "h", "hh", "hl", "pad")}
             for l in range(2)]

        block = ctx.enter_context(nc.Block())


        def load_tile(eng, n, s):
            wait(eng, w_lo, n - 1)
            eng.dma_start(Wraw[:, s, :], weights[bass.ds(n, 1)].rearrange("a p n -> p (a n)")).then_inc(w_in[s], 16)

        def split_hi(act, n_half, s, done, jobs):
            wait(act, done, jobs)
            act.wait_ge(w_in[s], 16 * (n_half + 1))
            act.activation(Wh[:, s, :], Wraw[:, s, :], ACT.Copy).then_inc(w_hi, 1)

        def split_lo(pool, n, s):
            pool.wait_ge(w_hi, n + 1)
            pool.tensor_tensor(Wl[:, s, :], Wraw[:, s, :], Wh[:, s, :].bitcast(F32), ALU.subtract).then_inc(w_lo, 1)

        def products(pe, ps, wh, wl, mh, ml, first, last):
            for w, m, begin in ((wh, mh, first), (wh, ml, False), (wl, mh, False)):
                for h in range(2):
                    ins = pe.matmul(ps[:, h * HALF:(h + 1) * HALF], w, m[:, h * HALF:(h + 1) * HALF],
                                    start=begin, stop=last and w is wl)
            return ins

        def full_job(pe, n, s, ps_slot, mh, ml, done, ready=None):
            pe.wait_ge(w_lo, n + 1)
            for kt in range(KT):
                if ready is not None:
                    pe.wait_ge(ready[0], kt + 1)
                    pe.wait_ge(ready[1], kt + 1)
                c = slice(kt * P, (kt + 1) * P)
                ins = products(pe, slot(ps_slot), Wh[:, s, c], Wl[:, s, c], mh[:, kt, :], ml[:, kt, :],
                               kt == 0, kt == KT - 1)
            ins.then_inc(done, 1)

        def square_sum(pe, n):
            pe.wait_ge(N[n]["used"], KT - 1)
            for h in range(2):
                ins = pe.matmul(slot(3)[:, h * HALF:(h + 1) * HALF], ones[:, :], acc[:, h * HALF:(h + 1) * HALF],
                                start=True, stop=True)
            ins.then_inc(N[n]["sum"], 1)

        def x_ready(eng, n, kt):
            if n == 0:
                eng.wait_ge(x_in_sem[kt], 16)
            else:
                eng.wait_ge(N[n]["x"], kt + 1)

        def norm_hi(act, n, kt):
            x_ready(act, n, kt)
            act.activation(XGh[:, kt, :], X[:, kt, :], ACT.Copy, scale=gcol(n, kt)).then_inc(N[n]["hi"], 1)

        def norm_square(act, n, kt):
            x_ready(act, n, kt)
            wait(act, N[n]["used"], kt - 2)
            dst = acc[:, :] if kt == 0 else sq[:, kt % 2, :]
            act.activation(dst, X[:, kt, :], ACT.Square).then_inc(N[n]["sq"], 1)

        def norm_act(act, n, kt):
            if n < 4:
                norm_hi(act, n, kt)
            norm_square(act, n, kt)

        def norm_lo(dve, n, kt):
            dve.wait_ge(N[n]["hi"], kt + 1)
            dve.scalar_tensor_tensor(out=XGl[:, kt, :], in0=X[:, kt, :], scalar=gcol(n, kt),
                                     in1=XGh[:, kt, :].bitcast(F32), op0=ALU.mult, op1=ALU.subtract
                                     ).then_inc(N[n]["lo"], 1)

        def norm_sum(eng, n, kt):
            eng.wait_ge(N[n]["sq"], kt + 1)
            wait(eng, N[n]["used"], kt - 1)
            eng.tensor_tensor(acc[:, :], acc[:, :], sq[:, kt % 2, :], ALU.add).then_inc(N[n]["used"], 1)

        def norm_factor(act, n):
            act.preload_act_table_set("natural_log_exp_and_others")
            act.wait_ge(N[n]["sum"], 1)
            act.activation(R[:, :], slot(3), ACT.Ln, bias=epsb[:, 0:1], scale=1.0 / D).then_inc(N[n]["read"], 1)
            act.wait_ge(N[n]["read"], 1)
            act.activation(R[:, :], R[:, :], ACT.Exp, scale=-0.5).then_inc(N[n]["r"], 1)

        def ffn_col(l, g, ht, kind, c):
            k = C_FFN + ((l * FT + ht) * 2 + kind) * 4 + c
            return par[:, k:k + 1] if is_first(g) else par[:, bass.ds(g * 16 + k, 1)]

        def conv_col(ft, c):
            return par[:, bass.ds(ft * 3 + (C_CONV + c), 1)]

        def lagged(q, first, tail):
            return (not first or q >= 0) and (not tail or q < QT)

        def on(q, first, tail):
            return q % 2 == 0 and lagged(q, first, tail)

        def run_steps(eng, step, last):
            for ii in range(QT):
                step(0, ii, first=True, parity=0)
            with eng.Fori(0, HEADS // 2 - 1) as pair:
                for a in range(2):
                    for ii in range(QT):
                        step(pair * 2 + (1 + a), ii, parity=1 - a)
            for ii in range(QT):
                step(HEADS - 1, ii, parity=1)
            for ii in range(QT, last + 1):
                step(HEADS - 1, ii, tail=True, parity=1)

        LAST = GROUPS - 1

        def up_job(g, j, first):
            return j if first else 4 + (g - 1) * 12 + (0, 9, 10, 11)[j]

        def up_tile(g, j, first):
            return j if first else 4 + (g - 1) * 6 + (0, 3, 4, 5)[j]

        def down_job(g, m, final):
            return 4 + g * 12 + m + (0 if final else 1)

        def down_tile(g, d, final):
            return 4 + g * 6 + d + (0 if final else 1)


        @block.sync
        def _(sp):
            sp.dma_start(X[:, 0, :], x_in[0]).then_inc(x_in_sem[0], 16)
            sp.dma_start(par[:, :], params_in).then_inc(small_in, 16)
            sp.dma_start(con[:, :], consts_in).then_inc(small_in, 16)
            load_tile(sp, 0, 0)
            sp.dma_start(lams, lams_in.partition_broadcast(P)).then_inc(small_in, 16)
            for kt in range(1, KT):
                sp.dma_start(X[:, kt, :], x_in[kt]).then_inc(x_in_sem[kt], 16)
            load_tile(sp, 1, 1)
            sp.wait_ge(N[0]["lo"], KT)
            sp.wait_ge(N[0]["sq"], KT)
            sp.dma_start(rot_a.bitcast(I32), positions.partition_broadcast(P)).then_inc(pos_in, 16)

            def whole(dram, h):
                return dram[bass.ds(h, 1)].rearrange("a p n -> p (a n)")

            def load_part(dst, dram, h, c, landed):
                for half in range(2):
                    sp.dma_start(dst[half * HD:(half + 1) * HD, :],
                                 dram[bass.ds(h, 1), c * HD:(c + 1) * HD, :].rearrange("a p n -> p (a n)")
                                 ).then_inc(landed, 16)

            def qkv_head(h, a):
                n = h * 3
                load_tile(sp, n + 2, a % 2)
                load_tile(sp, n + 3, (a + 1) % 2)
                load_tile(sp, n + 4, a % 2)
                sp.wait_ge(q_out, h + 1)
                sp.dma_start(whole(q_dram, h), q_res).then_inc(q_st, 16)
                sp.wait_ge(vt_out, h + 1)
                sp.dma_start(whole(v_dram, h), vt_res).then_inc(v_st, 16)
                sp.wait_ge(k_out, h + 1)
                sp.dma_start(whole(k_dram, h), k_res).then_inc(k_st, 16)

            for a in range(2):
                qkv_head(a, a)
            sp.wait_ge(N[0]["r"], 1)
            sp.wait_ge(k_st, 16)
            for c in range(2):
                load_part(land_first[c], k_dram, 0, c, first_in[0])
            sp.wait_ge(v_st, 16)
            sp.dma_start(land[4], whole(v_dram, 0)).then_inc(first_in[2], 16)
            for a in range(2):
                qkv_head(2 + a, a)
            sp.wait_ge(kl_made, 2)
            sp.wait_ge(q_st, 16)
            for c in range(2):
                load_part(land_first[c], q_dram, 0, c, first_in[1])
            with sp.Fori(2, HEADS // 2) as pair:
                for a in range(2):
                    qkv_head(pair * 2 + a, a)

            sp.wait_ge(k_st, 16 * HEADS)
            sp.wait_ge(q_st, 16 * HEADS)
            sp.wait_ge(v_st, 16 * HEADS)

            def load_k(h):
                for c in range(2):
                    sp.wait_ge(kl_made, 2 * h + c - 1)
                    load_part(land[c], k_dram, h, c, land_in[c])

            def load_q(h):
                for c in range(2):
                    sp.wait_ge(ql_made, 4 * h + c - 1)
                    load_part(land[2 + c], q_dram, h, c, land_in[2 + c])

            def load_v(h):
                sp.wait_ge(vl_made, 2 * h)
                sp.dma_start(land[4], whole(v_dram, h)).then_inc(land_in[4], 16)

            load_k(1)
            load_q(1)
            load_v(1)
            with sp.Fori(2, HEADS) as h:
                load_k(h)
                load_q(h)
                load_v(h)
            sp.wait_ge(kl_made, 2 * HEADS)
            sp.wait_ge(ql_made, 4 * HEADS)
            sp.dma_start(X[:, 4:8, :], x_in[4:8].rearrange("k p n -> p k n")).then_inc(x_again[1], 16)
            sp.wait_ge(t_done, HEADS * QT)
            sp.dma_start(X[:, 0:4, :], x_in[0:4].rearrange("k p n -> p k n")).then_inc(x_again[0], 16)
            with sp.Fori(T_WO // 2 + 1, T_END // 2) as pair:
                load_tile(sp, pair * 2, 0)
                load_tile(sp, pair * 2 + 1, 1)
            for kt in range(KT):
                sp.wait_ge(final_out, kt + 1)
                sp.dma_start(out[kt], X[:, kt, :]).then_inc(stored, 16)
            sp.wait_ge(stored, 16 * KT)


        @block.tensor
        def _(pe):
            def v_transpose(h):
                pe.wait_ge(v_out, h + 1)
                wait(pe, vt_out, h)
                for t in range(KT):
                    ins = pe.transpose(slot(3)[:, t * P:(t + 1) * P], v_res[:, t * P:(t + 1) * P], ident)
                ins.then_inc(vt_done, 1)

            def qkv_pair(pair, first):
                for a in range(2):
                    h = pair * 2 + a
                    n = pair * 6 + a * 3
                    wait(pe, v_out, h)
                    full_job(pe, n, a, 0, XGh, XGl, qkv_done,
                             (N[0]["hi"], N[0]["lo"]) if first and a == 0 else None)
                    wait(pe, rot_read, 2 * h - 1)
                    full_job(pe, n + 1, (a + 1) % 2, 1, XGh, XGl, qkv_done)
                    if first and a == 0:
                        square_sum(pe, 0)
                    wait(pe, rot_read, 2 * h)
                    full_job(pe, n + 2, a, 2, XGh, XGl, qkv_done)
                    if first and a == 0:
                        pe.wait_ge(N[0]["read"], 1)
                    v_transpose(h)

            pe.wait_ge(ones_set, 1)
            pe.wait_ge(small_in, 48)
            qkv_pair(0, True)
            with pe.Fori(1, HEADS // 2) as pair:
                qkv_pair(pair, False)

            def scores(h, i, q, parity):
                for c in range(2):
                    if q == 0:
                        pe.wait_ge(kl_made, 2 * h + c + 1)
                    if q % 4 == 0:
                        pe.wait_ge(ql_made, 4 * h + q // 2 + c + 1)
                    wait(pe, e_done, 2 * i + c - 1)
                    for half in range(2):
                        cols = slice(half * HALF, (half + 1) * HALF)
                        qs = Q_of(h)[c][:, q * P:(q + 1) * P]
                        pe.matmul(slot(c)[:, cols], qs, Kh[parity][c][:, cols], start=True, stop=False)
                        ins = pe.matmul(slot(c)[:, cols], qs, Kl[parity][c][:, cols], start=False, stop=True)
                    ins.then_inc(s_done, 1)

            def transposes(i, q):
                pe.wait_ge(a_done, i + 1)
                wait(pe, al_made, i)
                for t in range(KT):
                    ins = pe.transpose(slot(2)[:, t * P:(t + 1) * P], P1[q % 4][:, t * P:(t + 1) * P], ident)
                ins.then_inc(t_done, 1)

            def values(h, u, quarter, part):
                b = quarter % 2
                if part == 0:
                    pe.wait_ge(al_made, 2 * u + 2)
                    wait(pe, o_sq, u)
                if quarter == 0:
                    pe.wait_ge(vl_made, 2 * h + part + 1)
                for t in range(4 * part, 4 * part + 4):
                    c = slice(t * P, (t + 1) * P)
                    for w, m in ((0, Ah[b]), (0, Al[b]), (1, Ah[b])):
                        first, last = t == 0 and w == 0 and m is Ah[b], t == KT - 1 and w == 1
                        ins = pe.matmul(slot(3)[:, 0:2 * P], V[w][:, c], m[:, t, :], start=first, stop=last)
                ins.then_inc((pv_half, pv_done)[part], 1)

            def subln_sum(u, quarter):
                pe.wait_ge(o_sq, u + 1)
                pe.wait_ge(dg_done, 2 * u + 2)
                wait(pe, ln_done, u)
                pe.matmul(slot(3)[:, HALF:HALF + 2 * P], ones[:, :], osq, start=True, stop=False)
                for t in range(2):
                    b = 2 * quarter + t
                    ins = pe.matmul(slot(3)[:, HALF + t * P:HALF + (t + 1) * P], ones[:, :],
                                    dg[:, b * P:(b + 1) * P], start=False, stop=t == 1)
                ins.then_inc(ss_done, 1)

            def dense_ahead(a, kts):
                pe.wait_ge(w_lo, T_WO + a + 1)
                pe.wait_ge(e_done, 2 * HEADS * QT)
                for kt in kts:
                    pe.wait_ge(yh_made, 4 * kt + 4)
                    pe.wait_ge(yl_made, 4 * kt + 4)
                    c = slice(kt * P, (kt + 1) * P)
                    ins = products(pe, slot(a), Wh[:, a, c], Wl[:, a, c], Yh[:, kt, :], Yl[:, kt, :],
                                   kt == 0, kt == KT - 1)
                if kt == KT - 1:
                    ins.then_inc(dense_done[0], 1)

            def step(h, ii, first=False, tail=False, parity=0):
                i = h * QT + ii
                if not tail:
                    scores(h, i, ii, parity)
                if first and ii == 2:
                    pe.wait_ge(rot_read, 2 * HEADS)
                    pe.wait_ge(vt_out, HEADS)
                if lagged(ii - 2, first, tail):
                    transposes(i - 2, (ii - 2) % QT)
                if on(ii - 6, first, tail):
                    subln_sum(h * 4 + (ii - 6) // 2, (ii - 6) // 2 % 4)
                if on(ii - 4, first, tail):
                    values(h, h * 4 + (ii - 4) // 2, (ii - 4) // 2 % 4, 0)
                if on(ii - 5, first, tail):
                    values(h, h * 4 + (ii - 5) // 2, (ii - 5) // 2 % 4, 1)
                if tail:
                    dense_ahead(*((0, (0, 1)), (0, (2, 3)), (0, (4, 5, 6)), (1, (0, 1, 2)), (1, (3, 4, 5, 6)))[ii - QT])

            pe.wait_ge(v_out, HEADS)
            pe.wait_ge(rot_read, 2 * HEADS - 1)
            run_steps(pe, step, 12)

            def dense(d, base):
                def pair_of(pair):
                    for a in range(2):
                        n = pair * 2 + a
                        wait(pe, N[1 + 2 * d]["x"], n - 1)
                        full_job(pe, n + base, a, a, Yh, Yl, dense_done[d],
                                 (cyh, cyl) if isinstance(n, int) and n == 0 else None)
                if d == 0:
                    for a in range(2):
                        dense_ahead(a, (KT - 1,))
                else:
                    pair_of(0)
                with pe.Fori(1, KT // 2) as pair:
                    pair_of(pair)

            dense(0, T_WO)

            def ffn(l, base, norm):
                f = F[l]

                def up(g, j, first=False):
                    if not first:
                        pe.wait_ge(f["free"], up_job(g, j, first) - 3)
                    full_job(pe, up_tile(g, j, first) + base, j % 2, j, XGh, XGl, f["done"],
                             (N[norm]["hi"], N[norm]["lo"]) if first and j == 0 else None)

                def last_down_ahead():
                    pe.wait_ge(f["hh"], 2 * LAST + 1)
                    pe.wait_ge(f["hl"], 2 * LAST + 1)
                    pe.wait_ge(w_lo, base + down_tile(LAST, 0, True) + 1)
                    for m in range(4):
                        pe.wait_ge(f["free"], down_job(LAST, m, True) - 3)
                        c = slice(2 * m * P, (2 * m + 1) * P)
                        products(pe, slot(m), Wh[:, 0, c], Wl[:, 0, c], Hh[:, 0, :], Hl[:, 0, :], True, False)

                def down(g, final=False):
                    if final:
                        last_down_ahead()
                    pe.wait_ge(f["hh"], 2 * g + 2)
                    pe.wait_ge(f["hl"], 2 * g + 2)
                    for m in range(KT):
                        d, s = m // 4, (m // 4 + (0 if final else 1)) % 2
                        if m % 4 == 0:
                            pe.wait_ge(w_lo, base + down_tile(g, d, final) + 1)
                        ps = (m + (0 if final else 1)) % 4
                        if final and m >= 4:
                            pe.wait_ge(N[norm + 1]["x"], m - 3)
                        else:
                            pe.wait_ge(f["free"], down_job(g, m, final) - 3)
                        for k in ((1,) if final and m < 4 else (0, 1)):
                            c = slice((2 * (m % 4) + k) * P, (2 * (m % 4) + k + 1) * P)
                            ins = products(pe, slot(ps), Wh[:, s, c], Wl[:, s, c], Hh[:, k, :], Hl[:, k, :],
                                           k == 0, k == 1)
                        ins.then_inc(f["done"], 1)

                pe.wait_ge(N[norm]["x"], KT - 1)
                up(0, 0, True)
                square_sum(pe, norm)
                for j in (1, 2):
                    up(0, j, True)
                pe.wait_ge(N[norm]["read"], 1)
                up(0, 3, True)
                with pe.Fori(1, GROUPS) as g:
                    up(g, 0)
                    down(g - 1)
                    for j in (1, 2, 3):
                        up(g, j)
                down(LAST, True)

            ffn(0, T_FFN0, 1)

            def conv_pair(pair, first):
                for a in range(2):
                    for j in range(3):
                        n = pair * 6 + a * 3 + j
                        wait(pe, c_free, n - 2)
                        full_job(pe, n + T_CIN, (3 * a + j) % 2, j, XGh, XGl, c_done,
                                 (N[2]["hi"], N[2]["lo"]) if first and a == 0 and j == 0 else None)
                        if first and a == 0 and j == 0:
                            square_sum(pe, 2)

            pe.wait_ge(N[2]["x"], KT - 1)
            conv_pair(0, True)
            with pe.Fori(1, KT // 2) as pair:
                conv_pair(pair, False)
            pe.wait_ge(c_free, 3 * KT - 1)
            dense(1, T_COUT)
            ffn(1, T_FFN1, 3)
            square_sum(pe, 4)


        @block.scalar
        def _(act):
            def w_hi_static(n, done=None, jobs=0):
                split_hi(act, n // 2, n % 2, done, jobs)

            act.wait_ge(small_in, 48)
            act.wait_ge(ones_set, 1)
            norm_hi(act, 0, 0)
            w_hi_static(0)
            for kt in range(1, KT):
                norm_hi(act, 0, kt)
            w_hi_static(1)
            for kt in range(KT):
                norm_square(act, 0, kt)

            def qkv_pair(pair, first):
                for a in range(2):
                    h = pair * 2 + a
                    for j in range(3):
                        c = 3 * a + j
                        split_hi(act, pair * 3 + (c + 2) // 2, c % 2, qkv_done, pair * 6 + c + 1)
                        if first and c == 0:
                            norm_factor(act, 0)
                        if first and c == 1:
                            act.wait_ge(tab, 10)
                            act.activation(sin_r, sin_r, ACT.Sin).then_inc(sin_done, 1)
                            act.activation(cos_r, cos_r, ACT.Sin).then_inc(sin_done, 1)
                            act.wait_ge(lam_sum, 4)
                            act.activation(lam[:, 2:4], lam[:, 0:2], ACT.Exp).then_inc(lam_exp, 1)
                        if j == 2:
                            act.wait_ge(vt_done, h + 1)
                            wait(act, v_st, h * 16)
                            act.activation(vt_res, slot(3), ACT.Copy).then_inc(vt_out, 1)

            for pair in range(HEADS // 2):
                qkv_pair(pair, pair == 0)
                if pair == 1:
                    for c in range(2):
                        act.wait_ge(first_in[0], 64)
                        act.activation(Kh[0][c], land_first[c], ACT.Copy).then_inc(kh_made, 1)
                if pair == 2:
                    act.wait_ge(first_in[1], 64)
                    for part in range(2):
                        for c in range(2):
                            cols = slice(part * HALF, (part + 1) * HALF)
                            act.activation(Q_first[c][:, cols], land_first[c][:, cols], ACT.Copy, scale=-SCALE
                                           ).then_inc(qh_made, 1)

            act.preload_act_table_set("natural_log_exp_and_others")

            def k_hi(h, parity, c):
                if not (isinstance(h, int) and h == 1):
                    act.wait_ge(s_done, 16 * (h - 1))
                act.wait_ge(land_in[c], 32 * h)
                act.activation(Kh[parity][c], land[c], ACT.Copy).then_inc(kh_made, 1)

            def q_hi(h, c, part):
                cols = slice(part * HALF, (part + 1) * HALF)
                if not (isinstance(h, int) and h == 1):
                    act.wait_ge(s_done, 16 * h + c + 8 * part - 9)
                act.wait_ge(land_in[2 + c], 32 * h)
                act.activation(Q_later[c][:, cols], land[2 + c][:, cols], ACT.Copy, scale=-SCALE).then_inc(qh_made, 1)

            def v_hi(h, part):
                cols = slice(part * HALF, (part + 1) * HALF)
                wait(act, (pv_half, pv_done)[part], 4 * h)
                act.wait_ge(*((first_in[2], 16) if is_first(h) else (land_in[4], 16 * h)))
                act.activation(V[0][:, cols], land[4][:, cols], ACT.Copy).then_inc(vh_made, 1)

            def step(h, ii, first=False, tail=False, parity=0):
                i = h * QT + ii
                if lagged(ii - 2, first, tail):
                    q = (ii - 2) % QT
                    act.wait_ge(t_done, i - 1)
                    if q % 2 == 0:
                        wait(act, pv_done, h * 4 + (ii - 2) // 2 - 1)
                    act.activation(Ah[q // 2 % 2][:, :, q % 2 * P:(q % 2 + 1) * P],
                                   slot(2).rearrange("p (t n) -> p t n", n=P), ACT.Copy).then_inc(ah_made, 1)
                if not tail:
                    act.wait_ge(nb_done, 2 * i + 1)
                    wait(act, a_done, i - 1)
                    act.activation(P0[ii % 2], slot(0), ACT.Exp, bias=nb[:, 2 * (ii % 2):2 * (ii % 2) + 1],
                                   scale=-1.0, accum_out=rsum[:, 0, ii:ii + 1]).then_inc(e_done, 1)
                    act.wait_ge(nb_done, 2 * i + 2)
                    wait(act, t_done, i - 3)
                    act.activation(P1[ii % 4], slot(1), ACT.Exp, bias=nb[:, 2 * (ii % 2) + 1:2 * (ii % 2) + 2],
                                   scale=-1.0, accum_out=rsum[:, 1, ii:ii + 1]).then_inc(e_done, 1)
                if on(ii - 6, first, tail):
                    u = h * 4 + (ii - 6) // 2
                    act.wait_ge(ss_done, u + 1)
                    act.activation(z, slot(3)[:, HALF:HALF + 2 * P], ACT.Ln, scale=1.0 / VD).then_inc(ln_done, 1)
                    act.wait_ge(ln_done, u + 1)
                    act.activation(z, z, ACT.Exp, scale=-0.5).then_inc(z_done, 1)
                if on(ii - 5, first, tail):
                    u = h * 4 + (ii - 5) // 2
                    act.wait_ge(pv_done, u + 1)
                    wait(act, o_scaled, u)
                    act.activation(osb, slot(3)[:, 0:2 * P], ACT.Copy, scale=lam[:, 5:6]).then_inc(o_copied, 1)
                    wait(act, ss_done, u)
                    act.activation(osq, slot(3)[:, 0:2 * P], ACT.Square).then_inc(o_sq, 1)
                if on(ii - 8, first, tail):
                    u, uq = h * 4 + (ii - 8) // 2, (ii - 8) // 2
                    act.wait_ge(o_scaled, u + 1)
                    act.activation(Yh[:, bass.ds(h + uq // 4, 1), uq % 4 * 2 * P:(uq % 4 + 1) * 2 * P], ot3, ACT.Copy
                                   ).then_inc(yh_made, 1)
                if tail:
                    return
                if ii in (3, 4):
                    v_hi(h, ii - 3)
                if ii in (0, 1) and not first:
                    q_hi(h, ii, 1)
                if ii in (1, 2) and not is_last(h):
                    k_hi(h + 1, 1 - parity, ii - 1)
                if ii in (4, 5) and not is_last(h):
                    q_hi(h + 1, ii - 4, 0)

            act.wait_ge(lam_done, 2)
            run_steps(act, step, 14)

            def dense(d, base, norm):
                for kt in range(KT):
                    w_hi_static(base + kt + 2, dense_done[d], kt + 1)
                    norm_act(act, norm, kt)

            dense(0, T_WO, 1)

            def ffn(l, base, norm):
                f = F[l]

                def split_next(t_half, s, jobs):
                    split_hi(act, base // 2 + t_half, s, f["done"], jobs)

                def up(g, j, first):
                    t_off = j if first else (0, 3, 4, 5)[j]
                    t_half = (t_off + 2) // 2 if first else 2 + (g - 1) * 3 + (t_off + 2) // 2
                    split_next(t_half, t_off % 2, up_job(g, j, first) + 1)
                    if first and j == 0:
                        norm_factor(act, norm)
                    kind, ht = j % 2, j // 2
                    act.wait_ge(f["free"], up_job(g, j, first) + 1)
                    if kind == 0:
                        wait(act, f["h"], 2 * g + ht)
                        dst = Tg[:, :]
                    else:
                        wait(act, f["hl"], 2 * g + ht - 1)
                        dst = Tv[:, ht, :]
                    act.activation(dst, raws[kind][:, 1:S + 1], ACT.Identity, bias=ffn_col(l, g, ht, kind, 3),
                                   scale=ffn_col(l, g, ht, kind, 1)).then_inc(f["mid"], 1)
                    act.wait_ge(f["conv"], 4 * g + j + 1) if kind == 0 else None
                    if kind == 0:
                        act.activation(Tg[:, :], Tg[:, :], ACT.Silu).then_inc(f["silu"], 1)
                    else:
                        act.wait_ge(f["h"], 2 * g + ht + 1)
                        act.activation(Hh[:, ht, :], Tv[:, ht, :], ACT.Copy).then_inc(f["hh"], 1)

                for j in range(4):
                    up(0, j, True)
                with act.Fori(1, GROUPS) as g:
                    up(g, 0, False)
                    for d in range(2):
                        split_next(2 + (g - 1) * 3 + (3 + d) // 2, (1 + d) % 2, down_job(g - 1, 4 * d + 3, False) + 1)
                    for j in (1, 2, 3):
                        up(g, j, False)
                for m in range(KT):
                    if m % 4 == 3 and norm < 3:
                        w_hi_static(base + down_tile(LAST, m // 4, True) + 2, f["done"], down_job(LAST, m, True) + 1)
                    norm_act(act, norm + 1, m)

            ffn(0, T_FFN0, 1)

            def conv_pair(pair, first):
                for a in range(2):
                    ft = pair * 2 + a
                    for j in range(3):
                        c = 3 * a + j
                        split_hi(act, T_CIN // 2 + pair * 3 + (c + 2) // 2, c % 2, c_done, pair * 6 + c + 1)
                        if first and c == 0:
                            norm_factor(act, 2)
                        if j == 1:
                            act.wait_ge(cu_made, ft + 1)
                            act.activation(sq[:, 1, :], cu[:, 1:S + 1], ACT.Copy, scale=conv_col(ft, 1)).then_inc(ct_mid, 1)
                    act.wait_ge(cy_made, ft + 1)
                    act.activation(Yh[:, bass.ds(ft, 1), :], sq[:, 0:1, :], ACT.Copy).then_inc(cyh, 1)

            conv_pair(0, True)
            with act.Fori(1, KT // 2) as pair:
                conv_pair(pair, False)
            dense(1, T_COUT, 3)
            ffn(1, T_FFN1, 3)
            norm_factor(act, 4)


        @block.vector
        def _(dve):
            dve.memset(epsb[:, :], EPS)
            dve.memset(ones[:, :], 1.0).then_inc(ones_set, 1)
            dve.wait_ge(small_in, 48)
            for kt in range(KT):
                norm_lo(dve, 0, kt)
            for kt in range(1, KT):
                norm_sum(dve, 0, kt)

            def value_out(h):
                dve.wait_ge(qkv_done, 3 * h + 1)
                wait(dve, vt_done, h)
                dve.tensor_tensor(v_res, slot(0), R[:, :], ALU.mult).then_inc(v_out, 1)

            def tabled(count, ins):
                ins.then_inc(tab, 1)
                dve.wait_ge(tab, count)

            for c in range(2):
                pr = cu[:, 4 * HD + c * HD:4 * HD + (c + 1) * HD]
                dve.tensor_tensor(pr, lams[:, 2 * c * HD:(2 * c + 1) * HD], lams[:, (2 * c + 1) * HD:(2 * c + 2) * HD],
                                  ALU.mult).then_inc(lam_sum, 1)
                dve.wait_ge(lam_sum, 2 * c + 1)
                dve.reduce_sum(lam[:, c:c + 1], pr, axis=AX_X).then_inc(lam_sum, 1)
            dve.tensor_scalar(lam[:, 5:6], par[:, C_SUBG:C_SUBG + 1], 1.0 - LAMBDA_INIT, None, ALU.mult
                              ).then_inc(lam_done, 1)
            dve.wait_ge(pos_in, 16)
            ang, k_ = sin_r, cos_r
            tabled(1, dve.tensor_scalar(ang, rot_a.bitcast(I32), con[:, C_FREQ:C_FREQ + 1], None, ALU.mult))
            tabled(2, dve.tensor_scalar(k_, ang, 1.0 / (2.0 * np.pi), MAGIC, ALU.mult, ALU.add))
            tabled(3, dve.tensor_scalar(k_, k_, -MAGIC, None, ALU.add))
            for t in range(3):
                tabled(4 + t, dve.scalar_tensor_tensor(out=ang, in0=k_, scalar=-TWO_PI[t], in1=ang,
                                                       op0=ALU.mult, op1=ALU.add))
            tabled(7, dve.tensor_scalar(k_, ang, float(np.pi / 2), -2.0 * np.pi, ALU.is_gt, ALU.mult))
            tabled(8, dve.scalar_tensor_tensor(out=k_, in0=ang, scalar=float(np.pi / 2), in1=k_,
                                               op0=ALU.add, op1=ALU.add))
            tabled(9, dve.tensor_scalar(k_, k_, PI_IN, -PI_IN, ALU.min, ALU.max))
            tabled(10, dve.tensor_scalar(ang, ang, PI_IN, -PI_IN, ALU.min, ALU.max))
            dve.wait_ge(N[0]["r"], 1)
            value_out(0)
            dve.wait_ge(sin_done, 2)
            dve.wait_ge(lam_exp, 1)
            dve.scalar_tensor_tensor(out=lam[:, 4:5], in0=lam[:, 3:4], scalar=-LAMBDA_INIT, in1=lam[:, 2:3],
                                     op0=ALU.add, op1=ALU.subtract).then_inc(lam_done, 1)
            tabled(11, dve.tensor_tensor(cos_r, cos_r, R[:, :], ALU.mult))
            tabled(12, dve.scalar_tensor_tensor(out=sin_r, in0=sin_r, scalar=con[:, C_SIGN:C_SIGN + 1], in1=R[:, :],
                                                op0=ALU.mult, op1=ALU.mult))

            def rotate(n_done, n_rot, ps_slot, res, out_sem, h, st_sem, before, count):
                dve.wait_ge(qkv_done, n_done)
                wait(dve, before, count)
                dve.tensor_tensor(rot_a, slot(ps_slot), cos_r, ALU.mult).then_inc(rot_sum, 1)
                for q in range(4):
                    o, i = slice(32 * q, 32 * q + 32), slice(32 * (q ^ 1), 32 * (q ^ 1) + 32)
                    ins = dve.tensor_tensor(rot_b[o], slot(ps_slot)[i], sin_r[o], ALU.mult)
                ins.then_inc(rot_read, 1)
                dve.wait_ge(rot_sum, n_rot)
                dve.wait_ge(rot_read, n_rot)
                wait(dve, st_sem, h * 16)
                dve.tensor_tensor(res, rot_a, rot_b, ALU.add).then_inc(out_sem, 1)

            def qkv_head(h):
                if not is_first(h):
                    value_out(h)
                rotate(3 * h + 2, 2 * h + 1, 1, q_res, q_out, h, q_st, k_out, h)
                rotate(3 * h + 3, 2 * h + 2, 2, k_res, k_out, h, k_st, q_out, h + 1)

            def q_lo(h, c, part, src):
                up, cols = slice(HD, P), slice(part * HALF, (part + 1) * HALF)
                dve.wait_ge(qh_made, 4 * h + 2 * part + c + 1)
                dst = Q_of(h)[c][up, cols]
                dve.scalar_tensor_tensor(out=dst, in0=src[c][up, cols], scalar=-SCALE, in1=dst.bitcast(F32),
                                         op0=ALU.mult, op1=ALU.subtract).then_inc(ql_made, 1)

            qkv_head(0)
            with dve.Fori(1, 6) as h:
                qkv_head(h)
            for part in range(2):
                for c in range(2):
                    q_lo(0, c, part, land_first)
            with dve.Fori(6, HEADS) as h:
                qkv_head(h)

            dve.wait_ge(lam_done, 2)

            def minimum(i, ii, c):
                b = 2 * (ii % 2) + c
                dve.wait_ge(s_done, 2 * i + c + 1)
                dve.tensor_reduce(nb[:, b:b + 1], slot(c), axis=AX_X, op=ALU.min).then_inc(nb_done, 1)

            def step(h, ii, first=False, tail=False, parity=0):
                i = h * QT + ii
                if not tail:
                    minimum(i, ii, 0)
                if lagged(ii - 1, first, tail):
                    dve.wait_ge(e_done, 2 * i)
                    wait(dve, co_done, 2 * i - 2)
                    dve.reciprocal(coef[:, 0:1], rsum[:, 1, (ii - 1) % QT:(ii - 1) % QT + 1]).then_inc(inv_done, 1)
                if not tail:
                    minimum(i, ii, 1)
                if lagged(ii - 1, first, tail):
                    q = (ii - 1) % QT
                    dve.wait_ge(co_done, 2 * i)
                    dve.scalar_tensor_tensor(out=P1[q % 4], in0=P1[q % 4], scalar=coef[:, 3:4],
                                             in1=P0[q % 2], op0=ALU.mult, op1=ALU.add).then_inc(a_done, 1)
                if lagged(ii - 2, first, tail):
                    q = (ii - 2) % QT
                    cols = slice(q % 2 * P, (q % 2 + 1) * P)
                    dve.wait_ge(ah_made, i - 1)
                    dve.tensor_tensor(Al[q // 2 % 2][:, :, cols], slot(2).rearrange("p (t n) -> p t n", n=P),
                                      Ah[q // 2 % 2][:, :, cols].bitcast(F32), ALU.subtract).then_inc(al_made, 1)
                if ii in (1, 2) and not first:
                    q_lo(h, ii - 1, 1, land[2:4])
                if ii in (5, 6) and not is_last(h):
                    q_lo(h + 1, ii - 5, 0, land[2:4])

            run_steps(dve, step, 9)

            def add_and_norm(kt, ps_slot, done, jobs, norm):
                dve.wait_ge(done, jobs)
                dve.tensor_tensor(X[:, kt, :], slot(ps_slot), X[:, kt, :], ALU.add).then_inc(N[norm]["x"], 1)
                if norm < 4 and kt:
                    norm_lo(dve, norm, kt - 1)
                elif norm == 4 and kt > 1:
                    norm_sum(dve, norm, kt - 1)

            dve.wait_ge(x_again[0], 16)
            dve.wait_ge(x_again[1], 16)
            for kt in range(KT):
                add_and_norm(kt, kt % 2, dense_done[0], kt + 1, 1)
            norm_lo(dve, 1, KT - 1)

            def ffn(l, norm):
                f = F[l]
                for t in (rawg, rawv):
                    dve.memset(t[:, 0:1], 0.0)
                    ins = dve.memset(t[:, S + 1:S + 2], 0.0)
                ins.then_inc(f["pad"], 1)
                dve.wait_ge(f["pad"], 1)
                dve.wait_ge(N[norm]["r"], 1)

                def up(g, j, first):
                    kind, ht = j % 2, j // 2
                    dve.wait_ge(f["done"], up_job(g, j, first) + 1)
                    raw = raws[kind]
                    dve.tensor_tensor(raw[:, 1:S + 1], slot(j), R[:, :], ALU.mult).then_inc(f["free"], 1)
                    T = Tg[:, :] if kind == 0 else Tv[:, ht, :]
                    dve.wait_ge(f["mid"], 4 * g + j + 1)
                    dve.scalar_tensor_tensor(out=T, in0=raw[:, 0:S], scalar=ffn_col(l, g, ht, kind, 0), in1=T,
                                             op0=ALU.mult, op1=ALU.add).then_inc(f["tap"], 1)
                    dve.wait_ge(f["tap"], 4 * g + j + 1)
                    dve.scalar_tensor_tensor(out=T, in0=raw[:, 2:S + 2], scalar=ffn_col(l, g, ht, kind, 2), in1=T,
                                             op0=ALU.mult, op1=ALU.add).then_inc(f["conv"], 1)
                    if kind == 1:
                        dve.wait_ge(f["conv"], 4 * g + j + 1)
                        dve.wait_ge(f["silu"], 2 * g + ht + 1)
                        dve.tensor_tensor(T, Tg[:, :], T, ALU.mult).then_inc(f["h"], 1)
                        dve.wait_ge(f["hh"], 2 * g + ht + 1)
                        dve.tensor_tensor(Hl[:, ht, :], T, Hh[:, ht, :].bitcast(F32), ALU.subtract
                                          ).then_inc(f["hl"], 1)

                for j in range(4):
                    up(0, j, True)
                with dve.Fori(1, GROUPS) as g:
                    up(g, 0, False)
                    for m in range(KT):
                        dve.wait_ge(f["done"], down_job(g - 1, m, False) + 1)
                        dve.tensor_tensor(X[:, m, :], slot((m + 1) % 4), X[:, m, :], ALU.add).then_inc(f["free"], 1)
                    for j in (1, 2, 3):
                        up(g, j, False)
                for m in range(KT):
                    add_and_norm(m, m % 4, f["done"], down_job(LAST, m, True) + 1, norm + 1)
                if norm < 3:
                    norm_lo(dve, norm + 1, KT - 1)

            ffn(0, 1)

            dve.memset(cu[:, 0:1], 0.0)
            dve.memset(cu[:, S + 1:S + 2], 0.0).then_inc(c_pad, 1)
            dve.wait_ge(c_pad, 1)
            dve.wait_ge(N[2]["r"], 1)

            def conv_tile(ft):
                n = ft * 3
                c_t, u_t, T = acc[:, :], sq[:, 0, :], sq[:, 1, :]
                dve.wait_ge(c_done, n + 1)
                dve.tensor_tensor(c_t, slot(0), R[:, :], ALU.mult).then_inc(c_free, 1)
                dve.wait_ge(c_done, n + 2)
                wait(dve, cyl, ft)
                dve.tensor_tensor(u_t, slot(1), R[:, :], ALU.mult).then_inc(c_free, 1)
                dve.wait_ge(c_free, n + 2)
                dve.tensor_tensor(cu[:, 1:S + 1], c_t, u_t, ALU.mult).then_inc(cu_made, 1)
                dve.wait_ge(ct_mid, ft + 1)
                for e, (off, tap) in enumerate(((0, 0), (2, 2))):
                    dve.scalar_tensor_tensor(out=T, in0=cu[:, off:off + S], scalar=conv_col(ft, tap), in1=T,
                                             op0=ALU.mult, op1=ALU.add).then_inc(ct_made, 1)
                    dve.wait_ge(ct_made, 2 * ft + e + 1)
                dve.wait_ge(c_done, n + 3)
                dve.tensor_tensor(c_t, slot(2), R[:, :], ALU.mult).then_inc(c_free, 1)
                dve.wait_ge(c_free, n + 3)
                dve.tensor_tensor(u_t, T, c_t, ALU.mult).then_inc(cy_made, 1)
                dve.wait_ge(cyh, ft + 1)
                dve.tensor_tensor(Yl[:, bass.ds(ft, 1), :], sq[:, 0:1, :], Yh[:, bass.ds(ft, 1), :].bitcast(F32),
                                  ALU.subtract).then_inc(cyl, 1)

            conv_tile(0)
            with dve.Fori(1, KT) as ft:
                conv_tile(ft)
            for kt in range(KT):
                add_and_norm(kt, kt % 2, dense_done[1], kt + 1, 3)
            norm_lo(dve, 3, KT - 1)
            ffn(1, 3)
            norm_sum(dve, 4, KT - 1)
            dve.wait_ge(N[4]["r"], 1)
            for kt in range(KT):
                dve.scalar_tensor_tensor(out=X[:, kt, :], in0=X[:, kt, :], scalar=gcol(4, kt), in1=R[:, :],
                                         op0=ALU.mult, op1=ALU.mult).then_inc(final_out, 1)


        @block.gpsimd
        def _(pool):
            split_lo(pool, 0, 0)
            split_lo(pool, 1, 1)

            def k_lo(h, parity, c, src):
                pool.wait_ge(kh_made, 2 * h + c + 1)
                pool.tensor_tensor(Kl[parity][c], src[c], Kh[parity][c].bitcast(F32), ALU.subtract).then_inc(kl_made, 1)

            def v_lo(h, part):
                cols = slice(part * HALF, (part + 1) * HALF)
                pool.wait_ge(vh_made, 2 * h + part + 1)
                pool.tensor_tensor(V[1][:, cols], land[4][:, cols], V[0][:, cols].bitcast(F32), ALU.subtract
                                   ).then_inc(vl_made, 1)

            for begin, end in ((1, 7), (7, T_WO // 2 + 1)):
                with pool.Fori(begin, end) as pair:
                    for a in range(2):
                        split_lo(pool, pair * 2 + a, a)
                for c in range(2):
                    if begin == 1:
                        k_lo(0, 0, c, land_first)

            pool.wait_ge(lam_done, 2)

            def step(h, ii, first=False, tail=False, parity=0):
                i = h * QT + ii
                if lagged(ii - 1, first, tail):
                    q = (ii - 1) % QT
                    pool.wait_ge(inv_done, i)
                    pool.tensor_tensor(coef[:, 1:2], coef[:, 0:1], lam[:, 4:5], ALU.mult).then_inc(co_done, 1)
                    pool.wait_ge(co_done, 2 * i - 1)
                    wait(pool, a_done, i - 1)
                    pool.tensor_tensor(coef[:, 3:4], coef[:, 1:2], rsum[:, 0, q:q + 1], ALU.mult).then_inc(co_done, 1)
                    wait(pool, dg_done, i - 1)
                    pool.tensor_tensor(coef[:, 2:3], rsum[:, 0, q:q + 1], rsum[:, 0, q:q + 1], ALU.mult
                                       ).then_inc(s0sq_done, 1)
                    pool.wait_ge(s0sq_done, i)
                    wait(pool, ss_done, h * 4 + (ii - 9) // 2 + 2)
                    pool.tensor_tensor(dg[:, q * P:(q + 1) * P], con[:, C_EPSI:C_EPSI + P],
                                       coef[:, 2:3].to_broadcast([P, P]), ALU.mult).then_inc(dg_done, 1)
                if on(ii - 9, first, tail):
                    u, uq = h * 4 + (ii - 9) // 2, (ii - 9) // 2
                    dst = bass.ds(h + uq // 4, 1), slice(uq % 4 * 2 * P, (uq % 4 + 1) * 2 * P)
                    pool.wait_ge(yh_made, u + 1)
                    pool.tensor_tensor(Yl[:, dst[0], dst[1]], ot3, Yh[:, dst[0], dst[1]].bitcast(F32), ALU.subtract
                                       ).then_inc(yl_made, 1)
                if on(ii - 7, first, tail):
                    u = h * 4 + (ii - 7) // 2
                    pool.wait_ge(z_done, u + 1)
                    wait(pool, yl_made, u)
                    pool.tensor_tensor(ot, osb, z, ALU.mult).then_inc(o_scaled, 1)
                if tail:
                    return
                if ii in (3, 4):
                    v_lo(h, ii - 3)
                if ii in (5, 6) and not is_last(h):
                    k_lo(h + 1, 1 - parity, ii - 5, land)

            run_steps(pool, step, 15)

            def dense(base, norm):
                for kt in range(KT):
                    split_lo(pool, base + kt + 2, kt % 2)
                    if kt:
                        norm_sum(pool, norm, kt)

            def ffn(base, norm):
                with pool.Fori((base + 2) // 2, (base + 2 * FT + 2 * GROUPS) // 2) as pair:
                    for a in range(2):
                        split_lo(pool, pair * 2 + a, a)
                for m in range(KT):
                    if m % 4 == 3 and norm < 3:
                        n = base + down_tile(LAST, m // 4, True) + 2
                        split_lo(pool, n, n % 2)
                    if m and norm < 3:
                        norm_sum(pool, norm + 1, m)

            dense(T_WO, 1)
            ffn(T_FFN0, 1)
            with pool.Fori((T_CIN + 2) // 2, (T_COUT + 2) // 2) as pair:
                for a in range(2):
                    split_lo(pool, pair * 2 + a, a)
            dense(T_COUT, 3)
            ffn(T_FFN1, 3)


def _up_tiles(w):
    n = w.shape[1] // P
    return w.reshape(KT, P, n, P).transpose(2, 1, 0, 3).reshape(n, P, D)


def _down_tiles(w):
    return w.reshape(GROUPS, 2, P, 2, 4, P).transpose(0, 3, 2, 4, 1, 5).reshape(GROUPS, 2, P, D)


def _ffn_tiles(w_up, w_down):
    up, down = _up_tiles(w_up), _down_tiles(w_down)
    gate, val = up[:FT], up[FT:]
    order = [gate[0], val[0], gate[1], val[1]]
    for g in range(1, GROUPS):
        order += [gate[2 * g], down[g - 1, 0], down[g - 1, 1], val[2 * g], gate[2 * g + 1], val[2 * g + 1]]
    return np.stack(order + [down[GROUPS - 1, 0], down[GROUPS - 1, 1]])


def kernel(x, positions, attn_norm_g, attn_w_qkv, attn_lambda_q1, attn_lambda_k1, attn_lambda_q2, attn_lambda_k2,
           attn_subln_g, attn_w_o, conv_norm_g, conv_w_in, conv_w, conv_w_out, ffn_norm_g, ffn_w_up, ffn_conv_w,
           ffn_conv_b, ffn_w_down, final_norm_g):
    import concourse.bacc as bacc
    from concourse.bass_utils import run_bass_kernel_spmd

    a = {k: np.asarray(v) for k, v in locals().items() if k not in ("bacc", "run_bass_kernel_spmd")}
    qkv = _up_tiles(a["attn_w_qkv"][0]).reshape(3, HEADS, P, D)
    qkv = np.stack([qkv[2], qkv[0], qkv[1]], axis=1).reshape(3 * HEADS, P, D)
    cin = _up_tiles(a["conv_w_in"][0]).reshape(3, KT, P, D)
    cin = np.stack([cin[1], cin[2], cin[0]], axis=1).reshape(3 * KT, P, D)
    weights = np.concatenate([
        qkv, _up_tiles(a["attn_w_o"][0]), _ffn_tiles(a["ffn_w_up"][0], a["ffn_w_down"][0]),
        cin, _up_tiles(a["conv_w_out"][0]), _ffn_tiles(a["ffn_w_up"][1], a["ffn_w_down"][1])])
    norms = np.stack([a["attn_norm_g"][0], a["ffn_norm_g"][0], a["conv_norm_g"][0], a["ffn_norm_g"][1],
                      a["final_norm_g"]]).reshape(5 * KT, P)
    taps = np.concatenate([a["ffn_conv_w"], a["ffn_conv_b"][:, None]], axis=1)
    taps = taps.reshape(2, 4, 2, FT, P).transpose(0, 3, 2, 1, 4).reshape(2 * FT * 2 * 4, P)
    conv = a["conv_w"][0].reshape(3, KT, P).transpose(1, 0, 2).reshape(KT * 3, P)
    params = np.concatenate([norms, taps, conv, a["attn_subln_g"]]).T
    lams = np.concatenate([a["attn_lambda_q1"][0], a["attn_lambda_k1"][0], a["attn_lambda_q2"][0],
                           a["attn_lambda_k2"][0]])
    freq = (np.float32(THETA) ** (-np.arange(0, HD, 2, dtype=np.float32) / np.float32(HD))).astype(np.float32)
    sign = np.repeat(np.array([-1, 1, -1, 1], np.float32), 32)
    consts = np.concatenate([np.tile(freq, 4)[:, None], sign[:, None], np.eye(P, dtype=np.float32),
                             np.eye(P, dtype=np.float32) * np.float32(VD * EPS)], axis=1)
    ins = {
        "x_tiles": a["x"][0].T.reshape(KT, P, S), "positions": a["positions"][0], "weights": weights,
        "params": params, "consts": consts, "lams": lams,
    }
    nc = bacc.Bacc("TRN2", target_bir_lowering=False, num_devices=1)
    arrays, args = {}, []
    for name, v in ins.items():
        arrays[name] = np.ascontiguousarray(v)
        args.append(nc.dram_tensor(name, v.shape, mybir.dt.from_np(v.dtype), kind="ExternalInput").ap())
    args.append(nc.dram_tensor("y_tiles", (KT, P, S), F32, kind="ExternalOutput").ap())
    build(nc, *args)
    r = run_bass_kernel_spmd(nc, [arrays], core_ids=[0])
    return np.ascontiguousarray(r.results[0]["y_tiles"].reshape(D, S).T[None])
```
